# Optimizing a Trainium2 kernel written in Bass

```python
import math
import jax, jax.numpy as jnp
from jax import lax
import numpy as np

D_MODEL = 1024
BATCH = 1
SEQ = 1024
DEPTH = 1
DEC_BATCH = 1
DEC_SEQ = 1024
PAST_LEN = 128

D_MIX = D_MODEL
HEAD_DIM = 64
N_Q_HEADS = 8
N_KV_HEADS = 2
D_ATT = N_Q_HEADS * HEAD_DIM
D_KV = N_KV_HEADS * HEAD_DIM
D_LRU = D_MIX - D_ATT
N_LRU_BLOCKS = 8
LRU_BLOCK = D_LRU // N_LRU_BLOCKS
CONV_W = 4
CONV_PAD_LEFT = 2
LRU_C = 8.0
D_IN = D_ATT + 2 * D_KV + 2 * D_LRU
SPLITS = (D_ATT, D_ATT + D_KV, D_ATT + 2 * D_KV, D_ATT + 2 * D_KV + D_LRU)
GRID_W = 64
ROPE_THETA = 10000.0
ROPE_FREQS = HEAD_DIM // 4
Q_BLOCK = 128
N_EXPERTS = 64
TOP_K = 6
N_GROUPS = 8
TOPK_GROUPS = 4
D_EXPERT = 256
D_SHARED = 256
ROUTED_SCALE = 2.5
MOE_BLOCK = 128
N_MOD = 6
EPS = 1e-6
DN_ALPHA = (2.0 * DEPTH) ** 0.25
DN_BETA = (8.0 * DEPTH) ** -0.25

kernel_name = 'hybrid_rglru_gqa_moe_encoder'

def ln_plain(x):
    xf = x.astype(jnp.float32)
    mu = jnp.mean(xf, axis=-1, keepdims=True)
    var = jnp.mean(jnp.square(xf - mu), axis=-1, keepdims=True)
    return ((xf - mu) * lax.rsqrt(var + EPS)).astype(x.dtype)

def ln_affine(x, g, b):
    xf = x.astype(jnp.float32)
    mu = jnp.mean(xf, axis=-1, keepdims=True)
    var = jnp.mean(jnp.square(xf - mu), axis=-1, keepdims=True)
    y = (xf - mu) * lax.rsqrt(var + EPS) * g.astype(jnp.float32) + b.astype(jnp.float32)
    return y.astype(x.dtype)

def rms_norm(x, g):
    xf = x.astype(jnp.float32)
    y = xf * lax.rsqrt(jnp.mean(jnp.square(xf), axis=-1, keepdims=True) + EPS) * g.astype(jnp.float32)
    return y.astype(x.dtype)

def axial_rope_tables(S):
    rows = S // GRID_W
    row_idx = jnp.repeat(jnp.arange(rows, dtype=jnp.float32), GRID_W)
    col_idx = jnp.tile(jnp.arange(GRID_W, dtype=jnp.float32), rows)
    inv_freq = ROPE_THETA ** (-jnp.arange(ROPE_FREQS, dtype=jnp.float32) / ROPE_FREQS)
    ang = jnp.stack([row_idx[:, None] * inv_freq, col_idx[:, None] * inv_freq], axis=1)
    return jnp.cos(ang), jnp.sin(ang)

def apply_rope(x, cos, sin):
    B, S, H, _ = x.shape
    xr = x.astype(jnp.float32).reshape(B, S, H, 2, 2, ROPE_FREQS)
    x1 = xr[..., 0, :]
    x2 = xr[..., 1, :]
    c = cos[None, :, None]
    s = sin[None, :, None]
    out = jnp.stack([x1 * c - x2 * s, x2 * c + x1 * s], axis=-2)
    return out.reshape(B, S, H, HEAD_DIM).astype(x.dtype)

def block_attention(q, k, v):
    B, S = q.shape[0], q.shape[1]
    nq = S // Q_BLOCK
    G = N_Q_HEADS // N_KV_HEADS
    qb = q.reshape(B, nq, Q_BLOCK, N_KV_HEADS, G, HEAD_DIM).transpose(1, 0, 3, 4, 2, 5)
    kt = k.transpose(0, 2, 1, 3)
    vt = v.transpose(0, 2, 1, 3)
    scale = HEAD_DIM ** -0.5

    def one_block(qblk):
        s = jnp.einsum('bkgqd,bksd->bkgqs', qblk, kt, preferred_element_type=jnp.float32) * scale
        p = jax.nn.softmax(s, axis=-1).astype(vt.dtype)
        return jnp.einsum('bkgqs,bksd->bkgqd', p, vt)

    o = lax.map(one_block, qb)
    return o.transpose(1, 0, 4, 2, 3, 5).reshape(B, S, D_ATT)

def centred_conv(x, w, b):
    S = x.shape[1]
    xp = jnp.pad(x, ((0, 0), (CONV_PAD_LEFT, CONV_W - 1 - CONV_PAD_LEFT), (0, 0)))
    out = xp[:, 0:S] * w[0]
    for j in range(1, CONV_W):
        out = out + xp[:, j:j + S] * w[j]
    return out + b

def _lin_combine(left, right):
    a_l, b_l = left
    a_r, b_r = right
    return a_l * a_r, a_r * b_l + b_r

def rglru_direction(xc, wa, ba, wx, bx, lam, reverse):
    B, S, _ = xc.shape
    xb = xc.reshape(B, S, N_LRU_BLOCKS, LRU_BLOCK)
    r = jax.nn.sigmoid((jnp.einsum('bsnc,ncd->bsnd', xb, wa).reshape(B, S, D_LRU) + ba).astype(jnp.float32))
    i = jax.nn.sigmoid((jnp.einsum('bsnc,ncd->bsnd', xb, wx).reshape(B, S, D_LRU) + bx).astype(jnp.float32))
    log_a = -LRU_C * r * jax.nn.softplus(-lam.astype(jnp.float32))
    a = jnp.exp(log_a)
    gain = jnp.sqrt(-jnp.expm1(2.0 * log_a))
    bterm = gain * i * xc.astype(jnp.float32)
    _, h = lax.associative_scan(_lin_combine, (a, bterm), axis=1, reverse=reverse)
    return h

def mixer(u, p):
    B, S, _ = u.shape
    proj = u @ p['w_in']
    q, k, v, xl, gl = jnp.split(proj, SPLITS, axis=-1)
    q = rms_norm(q.reshape(B, S, N_Q_HEADS, HEAD_DIM), p['q_norm_g'])
    k = rms_norm(k.reshape(B, S, N_KV_HEADS, HEAD_DIM), p['k_norm_g'])
    v = v.reshape(B, S, N_KV_HEADS, HEAD_DIM)
    cos, sin = axial_rope_tables(S)
    att = block_attention(apply_rope(q, cos, sin), apply_rope(k, cos, sin), v)
    xc = centred_conv(xl, p['conv_w'], p['conv_b'])
    h = (rglru_direction(xc, p['lru_wa'][0], p['lru_ba'][0], p['lru_wx'][0], p['lru_bx'][0], p['lru_lambda'][0], False)
         + rglru_direction(xc, p['lru_wa'][1], p['lru_ba'][1], p['lru_wx'][1], p['lru_bx'][1], p['lru_lambda'][1], True))
    lru = jax.nn.gelu(gl) * h.astype(u.dtype)
    merged = jnp.concatenate([rms_norm(att, p['attn_out_g']), rms_norm(lru, p['lru_out_g'])], axis=-1)
    return merged @ p['w_out']

def swiglu(x, w_in, w_out):
    g, up = jnp.split(x @ w_in, 2, axis=-1)
    return (jax.nn.silu(g) * up) @ w_out

def routed_experts(xt, idx, w, w_exp_in, w_exp_out):
    T = xt.shape[0]
    TK = T * TOP_K
    flat_e = idx.reshape(TK)
    flat_tok = jnp.repeat(jnp.arange(T, dtype=jnp.int32), TOP_K)
    flat_w = w.reshape(TK)
    order = jnp.argsort(flat_e)
    se = flat_e[order]
    stok = flat_tok[order]
    sw = flat_w[order]
    counts = jnp.bincount(flat_e, length=N_EXPERTS)
    padded = (counts + MOE_BLOCK - 1) // MOE_BLOCK * MOE_BLOCK
    pad_end = jnp.cumsum(padded)
    pad_start = pad_end - padded
    start = jnp.cumsum(counts) - counts
    dest = pad_start[se] + (jnp.arange(TK, dtype=jnp.int32) - start[se])
    P = ((TK + MOE_BLOCK - 1) // MOE_BLOCK + N_EXPERTS) * MOE_BLOCK
    nblk = P // MOE_BLOCK
    buf_tok = jnp.zeros((P,), jnp.int32).at[dest].set(stok)
    buf_w = jnp.zeros((P,), jnp.float32).at[dest].set(sw)
    blk_start = jnp.arange(nblk, dtype=jnp.int32) * MOE_BLOCK
    blk_e = jnp.minimum(jnp.sum(pad_end[None, :] <= blk_start[:, None], axis=1), N_EXPERTS - 1)

    def body(acc, blk):
        tok, gw, e = blk
        yb = swiglu(xt[tok], w_exp_in[e], w_exp_out[e]) * gw[:, None].astype(xt.dtype)
        return acc.at[tok].add(yb), None

    out, _ = lax.scan(body, jnp.zeros_like(xt),
                      (buf_tok.reshape(nblk, MOE_BLOCK), buf_w.reshape(nblk, MOE_BLOCK), blk_e))
    return out

def moe(u, p):
    B, S, D = u.shape
    T = B * S
    xt = u.reshape(T, D)
    scores = jax.nn.sigmoid((xt @ p['w_router']).astype(jnp.float32))
    choice = scores + p['router_bias'].astype(jnp.float32)
    grp = choice.reshape(T, N_GROUPS, N_EXPERTS // N_GROUPS)
    grp_score = jnp.sum(lax.top_k(grp, 2)[0], axis=-1)
    _, top_grp = lax.top_k(grp_score, TOPK_GROUPS)
    grp_mask = jnp.any(top_grp[:, :, None] == jnp.arange(N_GROUPS)[None, None, :], axis=1)
    expert_mask = jnp.repeat(grp_mask, N_EXPERTS // N_GROUPS, axis=1)
    _, idx = lax.top_k(jnp.where(expert_mask, choice, -jnp.inf), TOP_K)
    w = jnp.take_along_axis(scores, idx, axis=1)
    w = w / jnp.sum(w, axis=-1, keepdims=True) * ROUTED_SCALE
    routed = routed_experts(xt, idx, w, p['w_exp_in'], p['w_exp_out'])
    shared = swiglu(xt, p['w_sh_in'], p['w_sh_out'])
    return (routed + shared).reshape(B, S, D)

def encoder_layer(x, c, p):
    mod = jax.nn.silu(c) @ p['w_ada'] + p['b_ada']
    shift1, scale1, gate1, shift2, scale2, gate2 = [m[:, None, :] for m in jnp.split(mod, N_MOD, axis=-1)]
    u = ln_plain(x) * (1.0 + scale1) + shift1
    x = ln_affine(DN_ALPHA * x + gate1 * mixer(u, p), p['ln1_g'], p['ln1_b'])
    u = ln_plain(x) * (1.0 + scale2) + shift2
    x = ln_affine(DN_ALPHA * x + gate2 * moe(u, p), p['ln2_g'], p['ln2_b'])
    return x

def trunk(x, c, params):
    for l in range(DEPTH):
        p = {name: arr[l] for name, arr in params.items()}
        x = encoder_layer(x, c, p)
    return x

def setup_inputs(seed: int = 0) -> dict:
    key = jax.random.key(seed)
    ks = jax.random.split(key, 32)
    L = DEPTH

    def nrm(k, shape, scale):
        return jax.random.normal(k, shape, jnp.float32) * scale

    col = jnp.arange(D_IN)
    v_cols = (col >= D_ATT + D_KV) & (col < D_ATT + 2 * D_KV)
    w_in = nrm(ks[6], (L, D_MODEL, D_IN), D_MODEL ** -0.5) * jnp.where(v_cols, DN_BETA, 1.0)
    a0 = jax.random.uniform(ks[16], (L, 2, D_LRU), jnp.float32, 0.9, 0.999)
    return {
        'x_prompt': nrm(ks[0], (BATCH, SEQ, D_MODEL), 1.0),
        'x_sample': nrm(ks[1], (DEC_BATCH, DEC_SEQ, D_MODEL), 1.0),
        'c_prompt': nrm(ks[2], (BATCH, D_MODEL), 1.0),
        'c_sample': nrm(ks[3], (DEC_BATCH, D_MODEL), 1.0),
        'w_ada': nrm(ks[4], (L, D_MODEL, N_MOD * D_MODEL), D_MODEL ** -0.5),
        'b_ada': nrm(ks[5], (L, N_MOD * D_MODEL), 0.02),
        'w_in': w_in,
        'q_norm_g': 1.0 + nrm(ks[7], (L, HEAD_DIM), 0.1),
        'k_norm_g': 1.0 + nrm(ks[8], (L, HEAD_DIM), 0.1),
        'conv_w': nrm(ks[9], (L, CONV_W, D_LRU), CONV_W ** -0.5),
        'conv_b': nrm(ks[10], (L, D_LRU), 0.02),
        'lru_wa': nrm(ks[11], (L, 2, N_LRU_BLOCKS, LRU_BLOCK, LRU_BLOCK), LRU_BLOCK ** -0.5),
        'lru_ba': nrm(ks[12], (L, 2, D_LRU), 0.02),
        'lru_wx': nrm(ks[13], (L, 2, N_LRU_BLOCKS, LRU_BLOCK, LRU_BLOCK), LRU_BLOCK ** -0.5),
        'lru_bx': nrm(ks[14], (L, 2, D_LRU), 0.02),
        'lru_lambda': jnp.log(a0) - jnp.log1p(-a0),
        'attn_out_g': 1.0 + nrm(ks[17], (L, D_ATT), 0.1),
        'lru_out_g': 1.0 + nrm(ks[18], (L, D_LRU), 0.1),
        'w_out': nrm(ks[19], (L, D_MIX, D_MODEL), D_MIX ** -0.5 * DN_BETA),
        'ln1_g': 1.0 + nrm(ks[20], (L, D_MODEL), 0.1),
        'ln1_b': nrm(ks[21], (L, D_MODEL), 0.02),
        'w_router': nrm(ks[22], (L, D_MODEL, N_EXPERTS), D_MODEL ** -0.5),
        'router_bias': nrm(ks[23], (L, N_EXPERTS), 0.01),
        'w_exp_in': nrm(ks[24], (L, N_EXPERTS, D_MODEL, 2 * D_EXPERT), D_MODEL ** -0.5 * DN_BETA),
        'w_exp_out': nrm(ks[25], (L, N_EXPERTS, D_EXPERT, D_MODEL), D_EXPERT ** -0.5 * DN_BETA),
        'w_sh_in': nrm(ks[26], (L, D_MODEL, 2 * D_SHARED), D_MODEL ** -0.5 * DN_BETA),
        'w_sh_out': nrm(ks[27], (L, D_SHARED, D_MODEL), D_SHARED ** -0.5 * DN_BETA),
        'ln2_g': 1.0 + nrm(ks[28], (L, D_MODEL), 0.1),
        'ln2_b': nrm(ks[29], (L, D_MODEL), 0.02),
    }

def reference(x_prompt, x_sample, c_prompt, c_sample, w_ada, b_ada, w_in, q_norm_g, k_norm_g,
              conv_w, conv_b, lru_wa, lru_ba, lru_wx, lru_bx, lru_lambda, attn_out_g, lru_out_g,
              w_out, ln1_g, ln1_b, w_router, router_bias, w_exp_in, w_exp_out, w_sh_in, w_sh_out,
              ln2_g, ln2_b):
    params = {
        'w_ada': w_ada, 'b_ada': b_ada, 'w_in': w_in, 'q_norm_g': q_norm_g, 'k_norm_g': k_norm_g,
        'conv_w': conv_w, 'conv_b': conv_b, 'lru_wa': lru_wa, 'lru_ba': lru_ba, 'lru_wx': lru_wx,
        'lru_bx': lru_bx, 'lru_lambda': lru_lambda, 'attn_out_g': attn_out_g, 'lru_out_g': lru_out_g,
        'w_out': w_out, 'ln1_g': ln1_g, 'ln1_b': ln1_b, 'w_router': w_router, 'router_bias': router_bias,
        'w_exp_in': w_exp_in, 'w_exp_out': w_exp_out, 'w_sh_in': w_sh_in, 'w_sh_out': w_sh_out,
        'ln2_g': ln2_g, 'ln2_b': ln2_b,
    }
    y_prompt = trunk(x_prompt, c_prompt, params)
    y_sample = trunk(x_sample, c_sample, params)
    return (y_prompt, y_sample)


_drawn_inputs = setup_inputs


def setup_inputs(seed=0):
    import zlib

    import numpy as np

    out = dict(_drawn_inputs(seed))
    spreads = {}
    factors = {'q_norm_g': 8.0,
     'k_norm_g': 8.0,
     'conv_b': 4.611,
     'lru_ba': 46.72,
     'lru_bx': 32.702,
     'ln2_b': 2.94}
    for name, (base, spread) in spreads.items():
        noise = np.random.default_rng([zlib.crc32(name.encode()), seed]).standard_normal(out[name].shape)
        drawn = base * np.exp(spread * noise) if base else spread * noise
        out[name] = __import__('jax').numpy.asarray(drawn.astype(out[name].dtype))
    for name, factor in factors.items():
        out[name] = (out[name] * factor).astype(out[name].dtype)
    return out
```

```python
from contextlib import ExitStack

import numpy as np

import concourse.bass as bass
from concourse import mybir

F32 = mybir.dt.float32
I32 = mybir.dt.int32
U32 = mybir.dt.uint32
ALU = mybir.AluOpType
ACT = mybir.ActivationFunctionType
AX = mybir.AxisListType

P = 128
D = 1024
KD = D // P
NB = 2
SEQ = 1024
T = NB * SEQ
NT = T // P
HD = 64
NQ = 8
NKV = 2
NH = NQ + NKV
D_ATT = NQ * HD
D_KV = NKV * HD
D_LRU = 512
KL = D_LRU // P
D_QKV = D_ATT + 2 * D_KV
D_IN = D_QKV + 2 * D_LRU
N_MOD = 6
EPS = 1e-6
ALPHA = 2.0 ** 0.25
CONV_W = 4
LRU_C = 8.0
N_EXP = 64
TOP_K = 6
N_GRP = 8
TOP_GRP = 4
D_E = 256
ROUTED_SCALE = 2.5
GRID_W = 64
RING = 4
CUMS = RING + 1 + N_EXP + 1
ROPE_FREQS = HD // 4


def passed(eng, sem):
    eng.sem_inc(sem, 1)


class Chain:

    def __init__(self, eng, sem, trip=0, per=0, base=0):
        self.eng, self.sem, self.trip, self.per, self.base, self.n = eng, sem, trip, per, base, 0

    def __call__(self, ins):
        ins.then_inc(self.sem, 1)
        self.n += 1
        self.eng.wait_ge(self.sem, self.trip * self.per + self.base + self.n)

    def closed(self):
        assert self.n == self.per, (self.n, self.per)


def conditioning(nc, w_ada, b_ada, cT, mod_d, list_d, acc_d, u2_d):
    HALF = N_MOD * D // 2
    BANKS = HALF // 512
    used = []
    with ExitStack() as ctx:
        sb = lambda n, s, d=F32: ctx.enter_context(nc.sbuf_tensor(n, s, d))
        sem = lambda n: used.append(nc.alloc_semaphore(n)) or used[-1]
        w = sb("ada_w", [P, RING, HALF])
        c = sb("ada_c", [P, KD, NB])
        sc = sb("ada_silu_c", [P, KD, NB])
        bias = sb("ada_bias", [NB, 2, HALF])
        mod = sb("ada_mod", [NB, 2, HALF])
        acc = ctx.enter_context(nc.psum_tensor("ada_acc", [P, BANKS, 512], F32))
        small_in, w_in_ring, silu_done, slot_free, half_done, acc_free, mod_done, stored = (
            sem("ada_small_in"), [sem(f"ada_w_in{r}") for r in range(RING)], sem("ada_silu"), sem("ada_slot_free"), sem("ada_half_done"),
            sem("ada_acc_free"), sem("ada_mod_done"), sem("ada_stored"))
        fill = sb("ada_fill", [P, 512, 2], I32)
        every = sb("ada_every", [P, NT, 2], I32)
        zero = sb("ada_zero", [P, D])
        fills, lists_out = sem("ada_fills"), sem("ada_lists_out")
        block = ctx.enter_context(nc.Block())

        @block.gpsimd
        def _(pool):
            nc.gpsimd.memset(fill[:, :, 1:2], 0).then_inc(fills, 1)
            nc.gpsimd.iota(fill[:, :, 0:1], [[0, 4], [1, P], [0, 1]], base=T, channel_multiplier=0).then_inc(fills, 1)
            nc.gpsimd.memset(every[:, :, 1:2].bitcast(F32), 1.0).then_inc(fills, 1)
            nc.gpsimd.iota(every[:, :, 0:1], [[P, NT], [0, 1]], base=0, channel_multiplier=1).then_inc(fills, 1)
            nc.gpsimd.memset(zero[:], 0.0).then_inc(fills, 1)

        @block.sync
        def _(sp):
            sp.dma_start(c[:], cT).then_inc(small_in, 16)
            for b in range(NB):
                sp.dma_start(bias[b:b + 1, :, :], b_ada.rearrange("a (h n) -> a h n", h=2)).then_inc(small_in, 16)
            with sp.Fori(0, 2) as half:
                for k in range(KD):
                    sp.wait_ge(slot_free, half * KD + (k + 1))
                    sp.dma_start(w[:, k % RING, :], w_ada[k * P:(k + 1) * P, bass.ds(half * HALF, HALF)]).then_inc(w_in_ring[k % RING], 16)
            sp.wait_ge(mod_done, 2)
            sp.dma_start(mod_d, mod[:].rearrange("b h n -> b (h n)")).then_inc(stored, 16)
            sp.wait_ge(stored, 16)

        @block.scalar
        def _(act):
            act.wait_ge(small_in, 16 * (1 + NB))
            nc.scalar.activation(sc[:], c[:], ACT.Silu).then_inc(silu_done, 1)
            act.wait_ge(fills, 5)
            lists = list_d[0:N_EXP * T, :].rearrange("(h p r) c -> h p (r c)", p=P, r=512)
            for h in range(N_EXP * T // (P * 512)):
                act.dma_start(lists[h], fill[:].rearrange("p r c -> p (r c)")).then_inc(lists_out, 16)
            act.dma_start(list_d[N_EXP * T:, :].rearrange("(n p) c -> p n c", p=P), every[:]).then_inc(lists_out, 16)
            for n in range(NT + 1):
                act.dma_start(acc_d[n * P:(n + 1) * P, :], zero[:]).then_inc(lists_out, 16)
            act.dma_start(u2_d[T:, :], zero[:]).then_inc(lists_out, 16)
            act.wait_ge(lists_out, 16 * (NT + 5))

        @block.tensor
        def _(pe):
            pe.sem_inc(slot_free, RING)
            pe.wait_ge(silu_done, 1)
            with pe.Fori(0, 2) as half:
                pe.wait_ge(acc_free, half + 1)
                for k in range(KD):
                    pe.wait_ge(w_in_ring[k % RING], half * (16 * KD // RING) + 16 * (k // RING + 1))
                    for n in range(BANKS):
                        mm = nc.tensor.matmul(acc[0:NB, n, :], sc[:, k, :], w[:, k % RING, n * 512:(n + 1) * 512],
                                              start=(k == 0), stop=(k == KD - 1))
                    mm.then_inc(slot_free, 1)

        @block.vector
        def _(dve):
            dve.sem_inc(acc_free, 1)
            dve.wait_ge(small_in, 16 * (1 + NB))
            for half in range(2):
                dve.wait_ge(slot_free, RING + KD * (half + 1))
                nc.vector.tensor_tensor(mod[:, half, :].rearrange("b (n f) -> b n f", f=512), acc[0:NB, :, :],
                                        bias[:, half, :].rearrange("b (n f) -> b n f", f=512), ALU.add).then_inc(mod_done, 1)
                dve.wait_ge(mod_done, half + 1)
                dve.sem_inc(acc_free, 1)
    nc.clear_and_free_semaphores(used)
    nc.all_engine_barrier()


def input_projection(nc, x, w_in, mod_cols, rope, qk_gain, ident_d, xl_d, gl_d, keep, apart):
    GT = 4
    qT, kTp, v = keep
    with ExitStack() as ctx:
        sb = lambda n, s, d=F32: ctx.enter_context(nc.sbuf_tensor(n, s, d))
        ps = lambda n, s: ctx.enter_context(nc.psum_tensor(n, s, F32))
        sem = lambda n: ctx.enter_context(nc.semaphore(n))
        w = sb("ip_w", [P, KD, D_IN])
        ident = sb("ip_ident", [P, P])
        modc = sb("ip_modc", [P, 2, KD])
        scale1 = sb("ip_scale1", [P, KD])
        xg = sb("ip_x", [P, 2, GT, D])
        uT = sb("ip_uT", [P, 2, KD, GT * P])
        st = sb("ip_stats", [P, GT, 2, 6])
        mv = sb("ip_mv", [P, GT, 2])
        ve = sb("ip_ve", [P, GT])
        sd = sb("ip_sd", [P, GT])
        rstd = sb("ip_rstd", [P, GT])
        qkv = sb("ip_qkv", [P, 2, NH * HD])
        t1 = sb("ip_t1", [P, NH * HD])
        t2 = sb("ip_t2", [P, NH * HD])
        ss = sb("ip_ss", [P, NH])
        hs = sb("ip_hs", [P, NH])
        hr = sb("ip_hr", [P, NH])
        rot = sb("ip_rot", [P, 2, NH * HD])
        tab = sb("ip_rope", [P, SEQ // P, 2, HD])
        gain = sb("ip_gain", [P, NH * HD])
        stage = sb("ip_stage", [P, 2, GT * P])
        pT = ps("ip_pT", [P, 2, 512])
        pQ = ps("ip_pQ", [P, 512])
        pK = ps("ip_pK", [P, 512])
        pR = ps("ip_pR", [P, 2, 512])
        pF = ps("ip_pF", [P, 2, 512])

        const_in, w_loaded, modc_in, modc_free, x_in, x_free = (sem("ip_const_in"), sem("ip_w_loaded"), sem("ip_modc_in"),
                                                                sem("ip_modc_free"), [sem("ip_x_in0"), sem("ip_x_in1")], sem("ip_x_free"))
        scale_ready, kzero = sem("ip_scale_ready"), sem("ip_kzero")
        var_ready, sd_ready, xn_ready = sem("ip_var_ready"), sem("ip_sd_ready"), sem("ip_xn_ready")
        pT_ready, uT_ready, uT_free = sem("ip_pT_ready"), sem("ip_uT_ready"), sem("ip_uT_free")
        qkv_mm, qkv_ready, qkv_free, ms_ready, hs_ready = (sem("ip_qkv_mm"), sem("ip_qkv_ready"), sem("ip_qkv_free"), sem("ip_ms_ready"),
                                                           sem("ip_hs_ready"))
        rot_ready, rot_mm, rot_copied = sem("ip_rot_ready"), sem("ip_rot_mm"), sem("ip_rot_copied")
        feat_mm, feat_staged, stage_stored = sem("ip_feat_mm"), sem("ip_feat_staged"), [sem("ip_stage_stored0"), sem("ip_stage_stored1")]
        steps = sem("ip_dve_steps")
        block = ctx.enter_context(nc.Block())
        FEAT = 2 * KL

        @block.sync
        def _(sp):
            sp.dma_start(ident[:], ident_d).then_inc(const_in, 16)
            sp.dma_start(tab[:], rope).then_inc(const_in, 16)
            sp.dma_start(gain[:], qk_gain.partition_broadcast(P)).then_inc(const_in, 16)
            with sp.Fori(0, NB) as b:
                for h in range(2):
                    for f in range(FEAT):
                        sp.wait_ge(feat_staged, (b * 2 + h) * FEAT + (f + 3))
                        passed(sp, apart)
                        dst = (xl_d if f < KL else gl_d)[(f % KL) * P:(f % KL + 1) * P, bass.ds(b * SEQ + h * 512, 512)]
                        sp.dma_start(dst, stage[:, f % 2, :]).then_inc(stage_stored[f % 2], 16)
            for r in range(2):
                sp.wait_ge(stage_stored[r], 16 * (1 + NB * 2 * FEAT // 2))

        @block.gpsimd
        def _(pool):
            def rows(b, h):
                pool.dma_start(xg[:, h, :, :], x[bass.ds(b * SEQ + h * 512, 512), :].rearrange("(j p) d -> p j d", p=P)).then_inc(x_in[h], 16)

            rows(0, 0)
            nc.gpsimd.memset(kTp[:], 0.0).then_inc(kzero, 1)
            for k in range(KD):
                pool.dma_start(w[:, k, :], w_in[k * P:(k + 1) * P, :]).then_inc(w_loaded, 16)
            with pool.Fori(0, NB) as b:
                pool.wait_ge(modc_free, b + 1)
                passed(pool, apart)
                pool.dma_start(modc[:], mod_cols[b], allow_slow_non_contiguous=True).then_inc(modc_in, 16)
                pool.wait_ge(x_free, b * 2 + 2)
                passed(pool, apart)
                rows(b, 1)
                pool.wait_ge(x_free, b * 2 + 3)
                passed(pool, apart)
                rows((b + 1) % NB, 0)
            pool.wait_ge(x_in[0], 16 * (NB + 1))

        @block.vector
        def _(dve):
            dve.sem_inc(modc_free, 1)
            dve.sem_inc(rot_ready, 4)
            dve.wait_ge(const_in, 48)

            def normalise(step, b, h):
                g = b * 2 + h
                dve.wait_ge(x_in[h], b * 16 + 16)
                for j in range(GT):
                    for c in range(2):
                        i = nc.vector.bn_stats(st[:, j, c, :], xg[:, h, j, c * 512:(c + 1) * 512])
                step(i)
                passed(dve, apart)
                for j in range(GT):
                    i = nc.vector.bn_aggr(mv[:, j, :], st[:, j, :, :].rearrange("p a s -> p (a s)"))
                step(i)
                nc.vector.tensor_scalar(ve[:], mv[:, :, 1], EPS, None, ALU.add).then_inc(var_ready, 1)
                dve.wait_ge(sd_ready, g + 1)
                step(nc.vector.reciprocal(rstd[:], sd[:]))
                for j in range(GT):
                    nc.vector.tensor_scalar(xg[:, h, j, :], xg[:, h, j, :], mv[:, j, 0:1], rstd[:, j:j + 1],
                                            ALU.subtract, ALU.mult).then_inc(xn_ready, 1)

            normalise(Chain(dve, steps, 0, 3), 0, 0)
            with dve.Fori(0, NB) as b:
                step = Chain(dve, steps, b, 2 * (3 + GT * 7), 3)
                dve.wait_ge(modc_in, b * 16 + 16)
                nc.vector.tensor_scalar(scale1[:], modc[:, 1, :], 1.0, None, ALU.add).then_inc(scale_ready, 1)
                for h in range(2):
                    for j in range(GT):
                        s = j % 2
                        q = qkv[:, s, :]
                        heads = lambda a: a.rearrange("p (n d) -> p n d", d=HD)
                        dve.wait_ge(qkv_ready, ((b * 2 + h) * GT + j + 1) * 2)
                        dve.wait_ge(rot_ready, ((b * 2 + h) * GT + j) * 2 + 4)
                        step(nc.vector.tensor_tensor(t1[:], q, q, ALU.mult))
                        step(nc.vector.tensor_reduce(ss[:], heads(t1[:]), AX.X, ALU.add))
                        nc.vector.tensor_scalar(ss[:], ss[:], 1.0 / HD, EPS, ALU.mult, ALU.add).then_inc(ms_ready, 1)
                        dve.wait_ge(hs_ready, (b * 2 + h) * GT + (j + 1))
                        step(nc.vector.reciprocal(hr[:], hs[:]))
                        step(nc.vector.tensor_tensor(heads(t1[:]), heads(q), hr[:].unsqueeze(2).to_broadcast([P, NH, HD]), ALU.mult))
                        step(nc.vector.tensor_tensor(t1[:], t1[:], gain[:], ALU.mult))
                        ct = tab[:, h * GT + j, 0, :]
                        sn = tab[:, h * GT + j, 1, :]
                        halves = lambda a: a.rearrange("p (n s f) -> p n s f", s=2, f=ROPE_FREQS)
                        for s2 in range(2):
                            for ax in range(2):
                                o = ax * 32
                                i = nc.vector.tensor_tensor(
                                    heads(t2[:])[:, :, o + 16 * s2:o + 16 * s2 + 16], heads(t1[:])[:, :, o + 16 * (1 - s2):o + 16 * (1 - s2) + 16],
                                    sn[:, o + 16 * s2:o + 16 * s2 + 16].unsqueeze(1).to_broadcast([P, NH, 16]), ALU.mult)
                        step(i)
                        step(nc.vector.tensor_tensor(heads(t1[:]), heads(t1[:]), ct.unsqueeze(1).to_broadcast([P, NH, HD]), ALU.mult))
                        dve.wait_ge(rot_mm, (b * 2 + h) * GT + (j + 1))
                        qv = lambda a: a[:, 0:D_ATT].rearrange("p (g i d) -> p g i d", g=NKV, d=HD)
                        rv = rot[:, s, 0:D_ATT].rearrange("p (i g d) -> p g i d", g=NKV, d=HD)
                        nc.vector.tensor_tensor(rv, qv(t1[:]), qv(t2[:]), ALU.add).then_inc(rot_ready, 1)
                        nc.vector.tensor_tensor(rot[:, s, D_ATT:], t1[:, D_ATT:], t2[:, D_ATT:], ALU.add).then_inc(rot_ready, 1)
                        if j == 1:
                            normalise(step, b + h, 1 - h)
                step.closed()

        @block.scalar
        def _(act):
            act.sem_inc(qkv_free, 1)
            act.sem_inc(rot_copied, 1)
            act.sem_inc(uT_ready, 2)
            act.sem_inc(feat_staged, 2)
            for r in range(2):
                act.sem_inc(stage_stored[r], 16)
            act.wait_ge(kzero, 1)

            def deviations(g):
                act.wait_ge(var_ready, g + 1)
                nc.scalar.activation(sd[:], ve[:], ACT.Sqrt).then_inc(sd_ready, 1)

            deviations(0)
            with act.Fori(0, NB) as b:
                act.wait_ge(scale_ready, b + 1)
                for h in range(2):
                    act.wait_ge(uT_free, b * 2 + (h + 1))
                    for k in range(KD):
                        act.wait_ge(pT_ready, (b * 2 + h) * KD + (k + 1))
                        nc.scalar.activation(uT[:, h, k, :], pT[:, k % 2, :], ACT.Identity, bias=modc[:, 0, k:k + 1],
                                             scale=scale1[:, k:k + 1]).then_inc(uT_ready, 1)
                    if h == 1:
                        act.wait_ge(uT_ready, (b * 2 + (h + 1)) * KD + 2)
                        act.sem_inc(modc_free, 1)

                    def feature(f):
                        act.wait_ge(feat_mm, (b * 2 + h) * FEAT + (f + 1))
                        act.wait_ge(stage_stored[f % 2], ((b * 2 + h) * (FEAT // 2) + (f // 2 + 1)) * 16)
                        nc.scalar.activation(stage[:, f % 2, :], pF[:, f % 2, :], ACT.Copy).then_inc(feat_staged, 1)

                    def qkv_out(j):
                        s = j % 2
                        act.wait_ge(qkv_mm, (b * 2 + h) * GT + (j + 1))
                        act.wait_ge(rot_ready, ((b * 2 + h) * GT + (j + 1)) * 2)
                        nc.scalar.activation(qkv[:, s, 0:D_ATT], pQ[:], ACT.Copy).then_inc(qkv_ready, 1)
                        nc.scalar.activation(qkv[:, s, D_ATT:], pK[:, 0:D_KV], ACT.Copy).then_inc(qkv_ready, 1)
                        nc.scalar.activation(v[:, bass.ds(b * 8 + (h * GT + j), 1), :].rearrange("p a d -> p (a d)"), pK[:, D_KV:2 * D_KV], ACT.Copy).then_inc(qkv_free, 1)
                        act.wait_ge(ms_ready, (b * 2 + h) * GT + (j + 1))
                        nc.scalar.activation(hs[:], ss[:], ACT.Sqrt).then_inc(hs_ready, 1)

                    def rot_out(j):
                        act.wait_ge(rot_mm, (b * 2 + h) * GT + (j + 1) + 2)
                        tok = bass.ds(b * SEQ + (h * GT + j) * P, P)
                        nc.scalar.activation(qT[:, :, tok], pR[:, 0, :].rearrange("p (i t) -> p i t", t=P), ACT.Copy)
                        nc.scalar.activation(kTp[0:64, 0, tok], pR[0:64, 1, 0:P], ACT.Copy, scale=HD ** -0.5)
                        nc.scalar.activation(kTp[64:128, 1, tok], pR[64:128, 1, 0:P], ACT.Copy, scale=HD ** -0.5).then_inc(rot_copied, 1)

                    for j in range(GT):
                        qkv_out(j)
                        feature(2 * j)
                        feature(2 * j + 1)
                        if j == 1:
                            deviations(b * 2 + (h + 1))
                        if j:
                            rot_out(j - 1)
                    rot_out(GT - 1)

        @block.tensor
        def _(pe):
            pe.sem_inc(x_free, 2)
            pe.sem_inc(uT_free, 2)
            pe.sem_inc(rot_mm, 2)
            pe.wait_ge(const_in, 48)
            pe.wait_ge(w_loaded, 16 * KD)
            with pe.Fori(0, NB) as b:
                for h in range(2):
                    pe.wait_ge(xn_ready, (b * 2 + h + 1) * GT)
                    for k in range(KD):
                        pe.wait_ge(uT_ready, (b * 2 + h) * KD + (k + 1))
                        for j in range(GT):
                            t = nc.tensor.transpose(pT[:, k % 2, j * P:(j + 1) * P], xg[:, h, j, k * P:(k + 1) * P], ident[:])
                        t.then_inc(pT_ready, 1)
                    pe.wait_ge(uT_ready, (b * 2 + (h + 1)) * KD + 2)
                    pe.sem_inc(x_free, 1)

                    def qkv_mms(j):
                        pe.wait_ge(qkv_free, (b * 2 + h) * GT + (j + 1))
                        for k in range(KD):
                            nc.tensor.matmul(pQ[:], uT[:, h, k, j * P:(j + 1) * P], w[:, k, 0:D_ATT], start=(k == 0), stop=(k == KD - 1))
                        for k in range(KD):
                            m = nc.tensor.matmul(pK[:, 0:2 * D_KV], uT[:, h, k, j * P:(j + 1) * P], w[:, k, D_ATT:D_QKV],
                                                 start=(k == 0), stop=(k == KD - 1))
                        m.then_inc(qkv_mm, 1)

                    def feat_mms(f):
                        pe.wait_ge(feat_staged, (b * 2 + h) * FEAT + (f + 1))
                        for k in range(KD):
                            m = nc.tensor.matmul(pF[:, f % 2, :], w[:, k, D_QKV + f * P:D_QKV + (f + 1) * P], uT[:, h, k, :],
                                                 start=(k == 0), stop=(k == KD - 1))
                        m.then_inc(feat_mm, 1)

                    def rot_mms(j):
                        pe.wait_ge(rot_ready, ((b * 2 + h) * GT + (j + 1)) * 2 + 4)
                        pe.wait_ge(rot_copied, (b * 2 + h) * GT + (j + 1))
                        for i in range(4):
                            nc.tensor.transpose(pR[:, 0, i * P:(i + 1) * P], rot[:, j % 2, i * P:(i + 1) * P], ident[:])
                        nc.tensor.transpose(pR[:, 1, 0:P], rot[:, j % 2, D_ATT:D_ATT + P], ident[:]).then_inc(rot_mm, 1)

                    for j in range(GT):
                        qkv_mms(j)
                        feat_mms(2 * j)
                        feat_mms(2 * j + 1)
                        if j:
                            rot_mms(j - 1)
                    rot_mms(GT - 1)
                    pe.wait_ge(feat_staged, (b * 2 + (h + 1)) * FEAT + 2)
                    pe.sem_inc(uT_free, 1)


def rg_lru(nc, xl_d, gl_d, gate_w, chan, lruT, apart):
    TAPS, CB, BA, BX, LAM = 0, 4, 5, 7, 9
    with ExitStack() as ctx:
        sb = lambda n, s, d=F32: ctx.enter_context(nc.sbuf_tensor(n, s, d))
        sem = lambda n: ctx.enter_context(nc.semaphore(n))
        wg = sb("lru_wg", [P, 4, P])
        ch = sb("lru_ch", [P, 11])
        xl = sb("lru_xl", [P, NB, SEQ + CONV_W])
        gl = sb("lru_gl", [P, NB, SEQ])
        xc = sb("lru_xc", [P, 2, NB, SEQ])
        fore = sb("lru_fore", [P, 2, NB, SEQ])
        raw = sb("lru_raw", [P, NB, SEQ])
        i_ = sb("lru_i", [P, 2, NB, 2, SEQ])
        th = sb("lru_th", [P, NB, 2, SEQ])
        back = sb("lru_back", [P, NB, SEQ])
        sq = sb("lru_sq", [P, SEQ])
        sp_ = sb("lru_softplus", [P, 6, 2])
        rate = sb("lru_rate", [P, 2, 2])
        pg = ctx.enter_context(nc.psum_tensor("lru_pg", [P, 2, 2, SEQ], F32))

        prep_in, prep_free, gl_in, scan_free, pad_ready = (sem("lru_prep_in"), sem("lru_prep_free"), sem("lru_gl_in"), sem("lru_scan_free"),
                                                           sem("lru_pad_ready"))
        abs_ready, exp_ready, rate_ready = sem("lru_abs_ready"), sem("lru_exp_ready"), sem("lru_rate_ready")
        xc_ready, gate_mm, gate_read, decay_ready = sem("lru_xc_ready"), sem("lru_gate_mm"), sem("lru_gate_read"), sem("lru_decay_ready")
        gain2_ready, gain_ready, gelu_ready, done = sem("lru_gain2_ready"), sem("lru_gain_ready"), sem("lru_gelu_ready"), sem("lru_done")
        steps = sem("lru_dve_steps")
        block = ctx.enter_context(nc.Block())
        PREP, SCAN = 29, 18

        def of(buf, c, b, d):
            return buf[:, bass.ds(c % 2, 1), b, d, :].rearrange("p q t -> p (q t)")

        def forward_of(c, b):
            return fore[:, bass.ds(c % 2, 1), b, :].rearrange("p q t -> p (q t)")

        def gate_of(c, b, d):
            return raw[:, b, :] if d else forward_of(c, b)

        def decay_of(c, b, d):
            return back[:, b, :] if d else forward_of(c, b)

        def conv_of(c, b, cols=slice(0, SEQ)):
            return xc[:, bass.ds(c % 2, 1), b, cols].rearrange("p q t -> p (q t)")

        @block.sync
        def _(sp):
            def prep(c):
                sp.wait_ge(prep_free, c + 1)
                sp.dma_start(ch[:], chan[c]).then_inc(prep_in, 16)
                sp.dma_start(wg[:], gate_w[c]).then_inc(prep_in, 16)
                sp.dma_start(xl[:, :, 2:2 + SEQ], xl_d[bass.ds(c * P, P), :].rearrange("p (b t) -> p b t", b=NB)).then_inc(prep_in, 16)

            def gate_branch(c):
                sp.wait_ge(scan_free, c + 1)
                sp.dma_start(gl[:], gl_d[bass.ds(c * P, P), :].rearrange("p (b t) -> p b t", b=NB)).then_inc(gl_in, 16)

            prep(0)
            with sp.Fori(0, KL - 1) as c:
                prep(c + 1)
                gate_branch(c)
            gate_branch(KL - 1)

        @block.vector
        def _(dve):
            dve.sem_inc(prep_free, 1)
            dve.sem_inc(scan_free, 1)
            nc.vector.memset(xl[:, :, 0:2], 0.0).then_inc(pad_ready, 1)
            nc.vector.memset(xl[:, :, 2 + SEQ:], 0.0).then_inc(pad_ready, 1)
            dve.wait_ge(pad_ready, 2)
            col = lambda k: sp_[:, k, :]

            def convolve(step, c):
                dve.wait_ge(prep_in, c * 48 + 48)
                nc.vector.tensor_scalar(col(0), ch[:, LAM:LAM + 2], -1.0, None, ALU.mult).then_inc(pad_ready, 1)
                dve.wait_ge(pad_ready, c + 3)
                nc.vector.tensor_tensor(col(1), ch[:, LAM:LAM + 2], col(0), ALU.min).then_inc(abs_ready, 1)
                for b in range(NB):
                    step(nc.vector.tensor_scalar(conv_of(c, b), xl[:, b, 0:SEQ], ch[:, TAPS:TAPS + 1], ch[:, CB:CB + 1], ALU.mult, ALU.add))
                    for j in range(1, CONV_W):
                        s = nc.vector.scalar_tensor_tensor(conv_of(c, b), xl[:, b, j:j + SEQ], ch[:, TAPS + j:TAPS + j + 1], conv_of(c, b),
                                                           ALU.mult, ALU.add)
                        if j < CONV_W - 1:
                            step(s)
                    s.then_inc(xc_ready, 1)

            def decay_rates(step, c):
                dve.wait_ge(exp_ready, c + 1)
                step(nc.vector.tensor_scalar(col(3), col(2), 2.0, None, ALU.add))
                step(nc.vector.reciprocal(col(3), col(3)))
                step(nc.vector.tensor_tensor(col(3), col(3), col(2), ALU.mult))
                step(nc.vector.tensor_tensor(col(4), col(3), col(3), ALU.mult))
                step(nc.vector.tensor_scalar(col(5), col(4), 1.0 / 17, 1.0 / 15, ALU.mult, ALU.add))
                for n in (13, 11, 9, 7, 5, 3, 1):
                    step(nc.vector.tensor_tensor(col(5), col(5), col(4), ALU.mult))
                    step(nc.vector.tensor_scalar(col(5), col(5), 1.0 / n, None, ALU.add))
                step(nc.vector.tensor_tensor(col(5), col(5), col(3), ALU.mult))
                step(nc.vector.tensor_scalar(col(5), col(5), 2.0 * LRU_C, None, ALU.mult))
                step(nc.vector.tensor_scalar(col(0), col(0), 0.0, LRU_C, ALU.max, ALU.mult))
                step(nc.vector.tensor_tensor(rate[:, 0, :], col(5), col(0), ALU.add))
                nc.vector.tensor_scalar(rate[:, 1, :], rate[:, 0, :], -1.0, None, ALU.mult).then_inc(rate_ready, 1)
                dve.wait_ge(gate_read, (c + 1) * (NB * 4) + 4)
                dve.wait_ge(rate_ready, c + 1)
                dve.sem_inc(prep_free, 1)

            def gains(step, c):
                for b in range(NB):
                    for d in range(2):
                        dve.wait_ge(decay_ready, c * 4 * NB + min(2 * (2 * b + d) + 3, 4 * NB))
                        step(nc.vector.tensor_tensor(sq[:], decay_of(c, b, d), decay_of(c, b, d), ALU.mult))
                        nc.vector.scalar_tensor_tensor(th[:, b, d, :], sq[:], 1.0, th[:, b, d, :], ALU.add, ALU.mult).then_inc(gain2_ready, 1)
                        step(nc.vector.tensor_tensor(of(i_, c, b, d), of(i_, c, b, d), conv_of(c, b), ALU.mult))

            def scans(step, c):
                for b in range(NB):
                    for d in range(2):
                        dve.wait_ge(gain_ready, (c * NB + b) * 2 + (d + 1))
                        step(nc.vector.tensor_tensor(sq[:], of(i_, c, b, d), th[:, b, d, :], ALU.mult))
                        if d == 0:
                            step(nc.vector.tensor_tensor_scan(th[:, b, d, :], decay_of(c, b, d), sq[:], 0.0, ALU.mult, ALU.add))
                        else:
                            step(nc.vector.tensor_tensor_scan(th[:, b, d, ::-1], back[:, b, ::-1], sq[:, ::-1], 0.0, ALU.mult, ALU.add))
                    step(nc.vector.tensor_tensor(th[:, b, 0, :], th[:, b, 0, :], th[:, b, 1, :], ALU.add))
                    dve.wait_ge(gelu_ready, c * NB + (b + 1))
                    nc.vector.tensor_tensor(lruT[:, bass.ds(c, 1), b * SEQ:(b + 1) * SEQ].rearrange("p a t -> p (a t)"),
                                            th[:, b, 0, :], gl[:, b, :], ALU.mult).then_inc(done, 1)
                dve.wait_ge(done, (c + 1) * NB)
                dve.sem_inc(scan_free, 1)

            first = Chain(dve, steps, 0, PREP)
            convolve(first, 0)
            decay_rates(first, 0)
            first.closed()
            with dve.Fori(0, KL - 1) as c:
                step = Chain(dve, steps, c, PREP + SCAN, PREP)
                convolve(step, c + 1)
                gains(step, c)
                decay_rates(step, c + 1)
                scans(step, c)
                step.closed()
            last = Chain(dve, steps, KL - 1, PREP + SCAN, PREP)
            gains(last, KL - 1)
            scans(last, KL - 1)

        @block.tensor
        def _(pe):
            pe.sem_inc(gate_read, 4)
            with pe.Fori(0, KL) as c:
                pe.wait_ge(prep_in, c * 48 + 48)
                for b in range(NB):
                    pe.wait_ge(xc_ready, c * NB + (b + 1))
                    pe.wait_ge(gate_read, (c * NB + (b + 1)) * 4)
                    for d in range(2):
                        for g in range(2):
                            for t in range(2):
                                m = nc.tensor.matmul(pg[:, d, g, t * 512:(t + 1) * 512], wg[:, 2 * d + g, :], conv_of(c, b, slice(t * 512, (t + 1) * 512)),
                                                     start=True, stop=True)
                            m.then_inc(gate_mm, 1)

        @block.scalar
        def _(act):
            def small_exp(c):
                act.wait_ge(abs_ready, c + 1)
                nc.scalar.activation(sp_[:, 2, :], sp_[:, 1, :], ACT.Exp).then_inc(exp_ready, 1)

            def gates(c, buffers_used):
                if buffers_used:
                    act.wait_ge(scan_free, c)
                    act.wait_ge(decay_ready, c * 4 * NB)
                for b in range(NB):
                    for d in range(2):
                        for g, (dst, bias) in enumerate(((gate_of(c, b, d), BA), (of(i_, c, b, d), BX))):
                            act.wait_ge(gate_mm, (c * NB + b) * 4 + (2 * d + g + 1))
                            nc.scalar.activation(dst, pg[:, d, g, :], ACT.Sigmoid, bias=ch[:, bias + d:bias + d + 1]).then_inc(gate_read, 1)

            def decays(c):
                act.wait_ge(rate_ready, c + 1)
                act.wait_ge(scan_free, c + 1)
                act.wait_ge(gate_read, (c + 1) * (NB * 4) + 4)
                for n in range(2 * NB + 1):
                    if n:
                        act.wait_ge(decay_ready, c * 4 * NB + max(1, 2 * n - 2))
                    if n < 2 * NB:
                        b, d = n // 2, n % 2
                        nc.scalar.activation(th[:, b, d, :], gate_of(c, b, d), ACT.Tanh, scale=rate[:, 0, d:d + 1]).then_inc(decay_ready, 1)
                    else:
                        passed(act, apart)
                    if n:
                        b, d = (n - 1) // 2, (n - 1) % 2
                        nc.scalar.activation(decay_of(c, b, d), gate_of(c, b, d), ACT.Exp, scale=rate[:, 1, d:d + 1]).then_inc(decay_ready, 1)

            def roots(c):
                for b in range(NB):
                    for d in range(2):
                        act.wait_ge(gain2_ready, (c * NB + b) * 2 + (d + 1))
                        nc.scalar.activation(th[:, b, d, :], th[:, b, d, :], ACT.Sqrt).then_inc(gain_ready, 1)
                act.wait_ge(gl_in, c * 16 + 16)
                for b in range(NB):
                    nc.scalar.activation(gl[:, b, :], gl[:, b, :], ACT.Gelu_apprx_tanh).then_inc(gelu_ready, 1)

            small_exp(0)
            gates(0, False)
            with act.Fori(0, KL - 1) as c:
                decays(c)
                small_exp(c + 1)
                gates(c + 1, True)
                roots(c)
            decays(KL - 1)
            roots(KL - 1)


def attention_tiles(nc, x, mod_d, ln1_rows, w_out, w_router, router_bias, chan_gain, consts, x1_d, u2_d, keep, lruT, route, apart):
    qT, kTp, v = keep
    list_d, acc_d, count_d, block_d = route
    NHD = NQ
    GQ = NQ // NKV
    KT = SEQ // P
    with ExitStack() as ctx:
        sb = lambda n, s, d=F32: ctx.enter_context(nc.sbuf_tensor(n, s, d))
        ps = lambda n, s: ctx.enter_context(nc.psum_tensor(n, s, F32))
        sem = lambda n: ctx.enter_context(nc.semaphore("at_" + n))
        wo = sb("at_wo", [P, 2, GQ, D])
        wr = sb("at_wr", [P, KD, N_EXP])
        rb = sb("at_rb", [P, N_EXP])
        ln = sb("at_ln", [P, 2, D])
        cg = sb("at_cg", [P, 2, GQ])
        cst = sb("at_cst", [P, 3, P])
        iota = sb("at_iota", [P, N_EXP])
        mrow = sb("at_mrow", [P, 3, D])
        slots = sb("at_slots", [P, TOP_K], I32)
        entry = sb("at_entry", [P, TOP_K, 2], I32)
        tokf = sb("at_tokf", [P, 1])
        Msum = sb("at_Msum", [P, N_EXP])
        tok0 = sb("at_tok0", [P, 1])
        cumi = sb("at_cumi", [P, CUMS], I32)
        blk = sb("at_blk", [P, 4], I32)
        half = sb("at_half", [P, 1])
        qs = sb("at_qs", [P, GQ, P])
        vs = sb("at_vs", [P, KT, NKV * HD])
        ls = sb("at_ls", [P, GQ, P])
        lsq = sb("at_lsq", [P, GQ, P])
        rms = sb("at_rms", [P, P])
        diag = sb("at_diag", [P, 2, P])
        pr = sb("at_pr", [P, 2, SEQ])
        pT = sb("at_pT", [P, KT, GQ, P])
        aT = sb("at_aT", [P, GQ, P])
        asq = sb("at_asq", [P, GQ, P])
        nm = sb("at_nm", [P, NHD])
        rs = sb("at_rs", [P, NHD])
        rr = sb("at_rr", [P, NHD])
        sm = sb("at_sm", [P, 8])
        f = sb("at_f", [P, D])
        xt = sb("at_x", [P, D])
        st = sb("at_st", [P, 2, 6])
        mv = sb("at_mv", [P, 2, 2])
        uT = sb("at_uT", [P, KD, P])
        ez = sb("at_ez", [P, N_EXP])
        sg = sb("at_sg", [P, N_EXP])
        ch = sb("at_ch", [P, N_EXP])
        top = sb("at_top", [P, N_GRP, 8])
        gs = sb("at_gs", [P, 3, 8])
        gi = sb("at_gi", [P, 2, 8], U32)
        gf = sb("at_gf", [P, 2, 8])
        gm = sb("at_gm", [P, N_GRP])
        M = sb("at_M", [P, N_EXP])
        junk = sb("at_junk", [P, 2 * TOP_K, N_EXP])
        wk = sb("at_wk", [P, 8])
        rk = sb("at_rk", [P, N_EXP])
        rkk = sb("at_rkk", [P, 8])
        pS = ps("at_pS", [P, 2, SEQ])
        pX = ps("at_pX", [P, 2, 512])
        pO = ps("at_pO", [P, GQ, P])
        pB = ps("at_pB", [P, 512])
        R1, R2, V1, V2, VA, VL = range(6)
        LOG, RNK, SSA, SSL, BCA, BCL = 0, 64, 128, 129, 256, 384

        const_in, wo_in, once = sem("const_in"), sem("wo_in"), sem("once")
        x_in, m_in = sem("x_in"), sem("m_in")
        q_ready, v_ready, l_ready, lsq_ready, ssl_mm, ssl_read = (sem("q_ready"), sem("v_ready"), sem("l_ready"), sem("lsq_ready"),
                                                                 sem("ssl_mm"), sem("ssl_read"))
        rms_ready, diag_ready, rows_mm, bcl_read = sem("rms_ready"), sem("diag_ready"), sem("rows_mm"), sem("bcl_read")
        s_mm, max_ready, exp_ready, p_ready = sem("s_mm"), sem("max_ready"), sem("exp_ready"), sem("p_ready")
        t0_mm, t1_mm, t0_copied, t1_copied, pv_mm = sem("t0_mm"), sem("t1_mm"), sem("t0_copied"), sem("t1_copied"), sem("pv_mm")
        att_scaled, asq_ready, ssa_mm, ssa_read = sem("att_scaled"), sem("asq_ready"), sem("ssa_mm"), sem("ssa_read")
        p2_mm, p1_mm, f_ready, gated = sem("p2_mm"), sem("p1_mm"), sem("f_ready"), sem("gated")
        var1, rstd1, xn1, x1_ready, x1_stored, var2, rstd2, u2_ready, u2_stored = (
            sem("var1"), sem("rstd1"), sem("xn1"), sem("x1_ready"), sem("x1_stored"), sem("var2"), sem("rstd2"), sem("u2_ready"), sem("u2_stored"))
        ut_mm, ut_copied, log_mm, ez_ready, m_ready, rank_mm, rank_read = (sem("ut_mm"), sem("ut_copied"), sem("log_mm"), sem("ez_ready"),
                                                                          sem("m_ready"), sem("rank_mm"), sem("rank_read"))
        steps, psteps, lsteps = sem("dve_steps"), sem("pool_steps"), sem("lru_steps")
        tok0_ready = sem("tok0_ready")
        count_mm, tables_ready, tables_out = sem("count_mm"), sem("tables_ready"), sem("tables_out")
        slots_ready, listed = sem("slots_ready"), sem("listed")
        block = ctx.enter_context(nc.Block())

        def trips(eng, trip, tail):
            trip(0, 0, True)
            trip(1, 1, True)
            trip(2, 2, True)
            with eng.Fori(3, NT - 1) as t:
                trip(t, 3, True)
            trip(NT - 1, 3, False)
            tail(NT)

        @block.sync
        def _(sp):
            for dst, src in ((wr[:], w_router), (rb[:], router_bias.partition_broadcast(P)), (ln[:], ln1_rows.partition_broadcast(P)),
                             (cg[:], chan_gain), (cst[:], consts[0]), (iota[:], consts[1].partition_broadcast(P)), (tokf[:], consts[2])):
                sp.dma_start(dst, src).then_inc(const_in, 16)
            sp.dma_start(wo[:], w_out).then_inc(wo_in, 16)
            sp.sem_inc(x1_stored, 16)

            def tail(t):
                sp.wait_ge(x1_stored, t * 16)
                tok = (t - 1) * P
                sp.dma_start(xt[:], x[bass.ds(tok, P), :]).then_inc(x_in, 16)
                sp.dma_start(mrow[:], mod_d[bass.ds((t - 1) // KT, 1), 2 * D:5 * D].rearrange("a (n d) -> (a n) d", d=D).partition_broadcast(P)).then_inc(m_in, 16)
                sp.wait_ge(x1_ready, t)
                sp.dma_start(x1_d[bass.ds(tok, P), :], xt[:]).then_inc(x1_stored, 16)
                sp.wait_ge(u2_ready, t)
                sp.dma_start(u2_d[bass.ds(tok, P), :], f[:]).then_inc(u2_stored, 16)

            with sp.Fori(1, NT + 1) as t:
                tail(t)
            sp.wait_ge(x1_stored, 16 * NT + 16)
            sp.wait_ge(u2_stored, 16 * NT)
            sp.wait_ge(tables_ready, 4)
            sp.dma_start(count_d, cumi[0:1, :]).then_inc(tables_out, 16)
            sp.dma_start(block_d.rearrange("a (c p) -> p (a c)", p=P), blk[:], allow_slow_non_contiguous=True).then_inc(tables_out, 16)
            sp.wait_ge(tables_out, 32)

        @block.gpsimd
        def _(pool):
            nc.gpsimd.memset(half[:], -0.5).then_inc(once, 1)
            nc.gpsimd.memset(Msum[:], 0.0).then_inc(once, 1)
            nc.gpsimd.memset(cumi[:], 0).then_inc(once, 1)
            pool.wait_ge(once, 3)
            pool.wait_ge(const_in, 16 * 7)

            def rsqrt(dst, src):
                return nc.gpsimd.tensor_tensor(dst, src, half[:], ALU.pow)

            def queries(t):
                nc.gpsimd.tensor_copy(qs[:], qT[:, :, bass.ds(t * P, P)]).then_inc(q_ready, 1)

            def trip(t, prev, nxt):
                if prev:
                    tail_a(t)
                    pool.wait_ge(pv_mm, t * NKV)
                    passed(pool, apart)
                nc.gpsimd.tensor_copy(vs[:], v[:, bass.ds((t // KT) * KT, KT), :]).then_inc(v_ready, 1)
                pool.wait_ge(ssl_read, t + 1)
                rsqrt(sm[:, VL:VL + 1], sm[:, VL:VL + 1]).then_inc(rms_ready, 1)
                pstep = Chain(pool, lsteps, t, 1)
                if prev:
                    pool.wait_ge(p2_mm, t)
                    passed(pool, apart)
                pstep(nc.gpsimd.tensor_tensor(ls[:], lruT[:, :, bass.ds(t * P, P)], cg[:, 1, :].unsqueeze(2).to_broadcast([P, GQ, P]), ALU.mult))
                pstep.closed()
                if prev:
                    tail_b1(t)
                pool.wait_ge(bcl_read, t + 1)
                nc.gpsimd.tensor_tensor(ls[:], ls[:], rms[:].unsqueeze(1).to_broadcast([P, GQ, P]), ALU.mult).then_inc(l_ready, 1)
                if prev:
                    tail_b2(t)
                if nxt:
                    pool.wait_ge(s_mm, (t + 1) * NHD)
                    passed(pool, apart)
                    queries(t + 1)
                pool.wait_ge(ssa_read, t + 1)
                rsqrt(sm[:, VA:VA + 1], sm[:, VA:VA + 1]).then_inc(rms_ready, 1)
                if prev > 1:
                    scatter(t - 1)

            def tail_a(t):
                pool.wait_ge(f_ready, 2 * t)
                pool.wait_ge(m_in, t * 16)
                nc.gpsimd.tensor_tensor(f[:], f[:], mrow[:, 0, :], ALU.mult).then_inc(gated, 1)

            def tail_b1(t):
                step = Chain(pool, psteps, t - 1, 1)
                pool.wait_ge(var1, t)
                rsqrt(sm[:, R1:R1 + 1], sm[:, V1:V1 + 1]).then_inc(rstd1, 1)
                pool.wait_ge(xn1, t)
                step(nc.gpsimd.tensor_tensor(xt[:], xt[:], ln[:, 0, :], ALU.mult))
                nc.gpsimd.tensor_tensor(xt[:], xt[:], ln[:, 1, :], ALU.add).then_inc(x1_ready, 1)
                step.closed()

            def tail_b2(t):
                pool.wait_ge(var2, t)
                rsqrt(sm[:, R2:R2 + 1], sm[:, V2:V2 + 1]).then_inc(rstd2, 1)

            def scatter(n):
                pool.wait_ge(slots_ready, n)
                passed(pool, apart)
                for k in range(TOP_K):
                    nc.gpsimd.indirect_dma_start(list_d, bass.IndirectOffsetOnAxis(ap=slots[:, k:k + 1].bitcast(U32), axis=0),
                                                 entry[:, k, :], None).then_inc(listed, 16)

            def tail(t):
                tail_a(t)
                tail_b1(t)
                tail_b2(t)
                scatter(t - 1)
                scatter(t)
                pool.wait_ge(listed, 16 * TOP_K * NT)

            queries(0)
            trips(pool, trip, tail)

        @block.scalar
        def _(act):
            act.wait_ge(const_in, 16 * 7)

            def exps(t, n, prev):
                act.wait_ge(max_ready, t * NHD + (n + 1))
                if prev or n >= 2:
                    act.wait_ge(t1_mm, t * NHD + (n - 1))
                nc.scalar.activation(pr[:, n % 2, :], pS[:, n % 2, :], ACT.Exp, bias=nm[:, n:n + 1], accum_out=rs[:, n:n + 1]).then_inc(exp_ready, 1)

            def copy_t(t, n, prev):
                act.wait_ge(t0_mm, t * NHD + (n + 1))
                if n >= GQ or prev:
                    act.wait_ge(pv_mm, t * NKV + (n // GQ))
                nc.scalar.activation(pT[:, 0:KT // 2, n % GQ, :], pX[:, 0, :].rearrange("p (k q) -> p k q", q=P), ACT.Copy).then_inc(t0_copied, 1)
                act.wait_ge(t1_mm, t * NHD + (n + 1))
                nc.scalar.activation(pT[:, KT // 2:KT, n % GQ, :], pX[:, 1, :].rearrange("p (k q) -> p k q", q=P), ACT.Copy).then_inc(t1_copied, 1)

            def tail_u(t):
                act.wait_ge(ut_mm, t)
                for h in range(2):
                    nc.scalar.activation(uT[:, 4 * h:4 * h + 4, :], pX[:, h, :].rearrange("p (k q) -> p k q", q=P), ACT.Copy).then_inc(ut_copied, 1)

            def tail_l(t):
                act.wait_ge(log_mm, t)
                nc.scalar.activation(ez[:], pB[:, LOG:LOG + N_EXP], ACT.Exp, scale=-1.0).then_inc(ez_ready, 1)

            def trip(t, prev, nxt):
                if prev:
                    act.wait_ge(ssl_mm, t)
                nc.scalar.activation(lsq[:], lruT[:, :, bass.ds(t * P, P)], ACT.Square).then_inc(lsq_ready, 1)
                exps(t, 1, prev)
                for n in range(NHD):
                    copy_t(t, n, prev)
                    if n + 2 < NHD:
                        exps(t, n + 2, prev)
                    if nxt and n == 6:
                        exps(t + 1, 0, 1)
                    if prev and n == 4:
                        tail_u(t)
                    if prev and n == 5:
                        tail_l(t)
                act.wait_ge(pv_mm, (t + 1) * NKV)
                if prev:
                    act.wait_ge(ssa_mm, t)
                nc.scalar.activation(asq[:], pO[:], ACT.Square).then_inc(asq_ready, 1)
                act.wait_ge(p1_mm, t + 1)
                if prev:
                    act.wait_ge(u2_stored, t * 16)
                    act.wait_ge(ut_mm, t)
                nc.scalar.activation(f[:, 0:512], pS[:, 1, 0:512], ACT.Copy).then_inc(f_ready, 1)

            def tail(t):
                tail_u(t)
                tail_l(t)

            exps(0, 0, 0)
            trips(act, trip, tail)

        @block.vector
        def _(dve):
            dve.sem_inc(rank_read, 1)
            dve.wait_ge(const_in, 16 * 7)
            dve.wait_ge(once, 3)
            nc.vector.tensor_copy(tok0[:], tokf[:]).then_inc(tok0_ready, 1)
            dve.wait_ge(tok0_ready, 1)
            TAIL_N, TAIL_8 = 39, 5
            ext = {}

            def step(ins):
                ins.then_inc(steps, 1)
                ext["n"] += 1
                dve.wait_ge(steps, ext["trip"] * ext["per"] + ext["base"] + ext["n"])

            def maxs(t, n):
                dve.wait_ge(s_mm, t * NHD + (n + 1))
                nc.vector.tensor_reduce(nm[:, n:n + 1], pS[:, n % 2, :], AX.X, ALU.max, negate=True).then_inc(max_ready, 1)

            def scale_p(t, n):
                dve.wait_ge(exp_ready, t * NHD + (n + 1))
                step(nc.vector.reciprocal(rr[:, n:n + 1], rs[:, n:n + 1]))
                nc.vector.tensor_scalar(pr[:, n % 2, :], pr[:, n % 2, :], rr[:, n:n + 1], None, ALU.mult).then_inc(p_ready, 1)

            def ln_stats(which, var_col, done):
                for c in range(2):
                    i = nc.vector.bn_stats(st[:, c, :], xt[:, c * 512:(c + 1) * 512])
                step(i)
                passed(dve, apart)
                step(nc.vector.bn_aggr(mv[:, which, :], st[:].rearrange("p a s -> p (a s)")))
                nc.vector.tensor_scalar(sm[:, var_col:var_col + 1], mv[:, which, 1:2], EPS, None, ALU.add).then_inc(done, 1)

            def tail_1(t):
                dve.wait_ge(x_in, t * 16)
                dve.wait_ge(gated, t)
                step(nc.vector.scalar_tensor_tensor(xt[:], xt[:], ALPHA, f[:], ALU.mult, ALU.add))
                ln_stats(0, V1, var1)

            def tail_2(t):
                dve.wait_ge(rstd1, t)
                nc.vector.tensor_scalar(xt[:], xt[:], mv[:, 0, 0:1], sm[:, R1:R1 + 1], ALU.subtract, ALU.mult).then_inc(xn1, 1)

            def tail_3(t):
                dve.wait_ge(x1_ready, t)
                ln_stats(1, V2, var2)

            def tail_4(t):
                dve.wait_ge(rstd2, t)
                dve.wait_ge(m_in, t * 16)
                step(nc.vector.tensor_scalar(f[:], xt[:], mv[:, 1, 0:1], sm[:, R2:R2 + 1], ALU.subtract, ALU.mult))
                step(nc.vector.scalar_tensor_tensor(f[:], mrow[:, 2, :], 1.0, f[:], ALU.add, ALU.mult))
                nc.vector.tensor_tensor(f[:], f[:], mrow[:, 1, :], ALU.add).then_inc(u2_ready, 1)

            def tail_5(t):
                dve.wait_ge(ez_ready, t)
                step(nc.vector.tensor_scalar(ez[:], ez[:], 1.0, None, ALU.add))
                step(nc.vector.reciprocal(sg[:], ez[:]))
                step(nc.vector.tensor_tensor(ch[:], sg[:], rb[:], ALU.add))
                passed(dve, apart)
                for g in range(N_GRP):
                    i = nc.vector.max(top[:, g, :], ch[:, g * 8:g * 8 + 8])
                step(i)
                step(nc.vector.tensor_tensor(gs[:, 0, :], top[:, :, 0], top[:, :, 1], ALU.add))
                passed(dve, apart)
                step(nc.vector.max(gs[:, 1, :], gs[:, 0, :]))
                passed(dve, apart)
                step(nc.vector.max_index(gi[:, 0, :], gs[:, 1, :], gs[:, 0, :]))
                step(nc.vector.tensor_copy(gf[:, 0, :], gi[:, 0, :]))
                step(nc.vector.tensor_scalar(gm[:], iota[:, 0:N_GRP], gf[:, 0, 0:1], None, ALU.is_equal))
                for k in range(1, TOP_GRP):
                    step(nc.vector.scalar_tensor_tensor(gm[:], iota[:, 0:N_GRP], gf[:, 0, k:k + 1], gm[:], ALU.is_equal, ALU.add))

            def tail_6(t):
                step(nc.vector.tensor_scalar(gm[:], gm[:], -1.0, 1e30, ALU.add, ALU.mult))
                step(nc.vector.tensor_tensor(ch[:].rearrange("p (g e) -> p g e", e=8), ch[:].rearrange("p (g e) -> p g e", e=8),
                                             gm[:].unsqueeze(2).to_broadcast([P, N_GRP, 8]), ALU.add))
                passed(dve, apart)
                step(nc.vector.max(gs[:, 2, :], ch[:]))
                passed(dve, apart)
                step(nc.vector.max_index(gi[:, 1, :], gs[:, 2, :], ch[:]))
                step(nc.vector.tensor_copy(gf[:, 1, :], gi[:, 1, :]))
                step(nc.vector.tensor_scalar(M[:], iota[:], gf[:, 1, 0:1], None, ALU.is_equal))
                for k in range(1, TOP_K):
                    i = nc.vector.scalar_tensor_tensor(M[:], iota[:], gf[:, 1, k:k + 1], M[:], ALU.is_equal, ALU.add)
                    if k < TOP_K - 1:
                        step(i)
                i.then_inc(m_ready, 1)
                for k in range(TOP_K):
                    i = nc.vector.scalar_tensor_tensor(junk[:, k, :], iota[:], gf[:, 1, k:k + 1], sg[:], ALU.is_equal, ALU.mult,
                                                       accum_out=wk[:, k:k + 1])
                step(i)
                step(nc.vector.tensor_reduce(wk[:, 6:7], wk[:, 0:TOP_K], AX.X, ALU.add))
                step(nc.vector.reciprocal(wk[:, 7:8], wk[:, 6:7]))
                step(nc.vector.tensor_scalar(wk[:, 0:TOP_K], wk[:, 0:TOP_K], wk[:, 7:8], ROUTED_SCALE, ALU.mult, ALU.mult))

            def tail_7(t):
                dve.wait_ge(rank_mm, t)
                step(nc.vector.tensor_copy(rk[:], pB[:, RNK:RNK + N_EXP]))
                dve.sem_inc(rank_read, 1)

            def tail_8(t, wait):
                nc.vector.tensor_tensor(Msum[:], Msum[:], M[:], ALU.add)
                for k in range(TOP_K):
                    i = nc.vector.scalar_tensor_tensor(junk[:, TOP_K + k, :], iota[:], gf[:, 1, k:k + 1], rk[:], ALU.is_equal, ALU.mult,
                                                       accum_out=rkk[:, k:k + 1])
                step(i)
                step(nc.vector.scalar_tensor_tensor(rkk[:, 0:TOP_K], gf[:, 1, 0:TOP_K], float(T), rkk[:, 0:TOP_K], ALU.mult, ALU.add))
                if wait:
                    dve.wait_ge(listed, 16 * TOP_K * (t - 1))
                step(nc.vector.tensor_copy(entry[:, :, 1].bitcast(F32), wk[:, 0:TOP_K]))
                step(nc.vector.tensor_copy(entry[:, :, 0], tokf[:].to_broadcast([P, TOP_K])))
                step(nc.vector.tensor_scalar(tokf[:], tokf[:], float(P), None, ALU.add))
                nc.vector.tensor_copy(slots[:], rkk[:, 0:TOP_K]).then_inc(slots_ready, 1)

            HEAD_STEPS = NHD + 1
            BEFORE_1 = 1 + HEAD_STEPS
            BEFORE_2 = BEFORE_1 + HEAD_STEPS + TAIL_N - TAIL_8
            PER = HEAD_STEPS + TAIL_N

            def trip(t, prev, nxt):
                base, here = ((1, HEAD_STEPS), (BEFORE_1, PER - TAIL_8), (BEFORE_2 - 2 * PER, PER))[min(prev, 2)]
                ext.update(trip=t, per=PER if prev > 1 else 0, base=base, n=0)
                maxs(t, 1)
                for n in range(NHD):
                    if n + 1 < NHD:
                        scale_p(t, n + 1)
                    elif nxt:
                        scale_p(t + 1, 0)
                    if n + 2 < NHD:
                        maxs(t, n + 2)
                    elif nxt and n == 6:
                        maxs(t + 1, 0)
                    if n == 1:
                        dve.wait_ge(ssl_mm, t + 1)
                        nc.vector.tensor_scalar(sm[:, VL:VL + 1], pB[:, SSL:SSL + 1], 1.0 / D_LRU, EPS, ALU.mult, ALU.add).then_inc(ssl_read, 1)
                    if n == 2:
                        dve.wait_ge(rms_ready, 2 * t + 1)
                        nc.vector.tensor_scalar(diag[:, 1, :], cst[:, 0, :], sm[:, VL:VL + 1], None, ALU.mult).then_inc(diag_ready, 1)
                    if n == 3:
                        dve.wait_ge(rows_mm, 2 * t + 1)
                        if prev:
                            dve.wait_ge(l_ready, t)
                        nc.vector.tensor_copy(rms[:], pB[:, BCL:BCL + P]).then_inc(bcl_read, 1)
                    if prev:
                        for piece in {0: (tail_1,), 1: (tail_2,), 3: (tail_3, tail_4)}.get(n, ()):
                            piece(t)
                if prev > 1:
                    tail_8(t - 1, prev > 2)
                dve.wait_ge(pv_mm, (t + 1) * NKV)
                if prev:
                    dve.wait_ge(p1_mm, t)
                dve.wait_ge(asq_ready, t + 1)
                step(nc.vector.tensor_tensor(aT[:], pO[:], cg[:, 0, :].unsqueeze(2).to_broadcast([P, GQ, P]), ALU.mult))
                dve.wait_ge(ssa_mm, t + 1)
                nc.vector.tensor_scalar(sm[:, VA:VA + 1], pB[:, SSA:SSA + 1], 1.0 / D_ATT, EPS, ALU.mult, ALU.add).then_inc(ssa_read, 1)
                dve.wait_ge(rms_ready, 2 * t + 2)
                nc.vector.tensor_scalar(diag[:, 0, :], cst[:, 0, :], sm[:, VA:VA + 1], None, ALU.mult).then_inc(diag_ready, 1)
                dve.wait_ge(rows_mm, 2 * t + 2)
                nc.vector.tensor_tensor(aT[:], aT[:], pB[:, BCA:BCA + P].unsqueeze(1).to_broadcast([P, GQ, P]), ALU.mult).then_inc(att_scaled, 1)
                if prev:
                    tail_5(t)
                    tail_6(t)
                dve.wait_ge(p1_mm, t + 1)
                if prev:
                    dve.wait_ge(u2_stored, t * 16)
                    dve.wait_ge(ut_mm, t)
                nc.vector.tensor_copy(f[:, 512:], pS[:, 1, 512:]).then_inc(f_ready, 1)
                if prev:
                    tail_7(t)
                assert ext["n"] == here - (0 if nxt else 1), (ext["n"], here)

            def tail(t):
                ext.update(trip=0, per=0, base=BEFORE_2 + (NT - 2) * PER - 1, n=0)
                tail_8(t - 1, True)
                for piece in (tail_1, tail_2, tail_3, tail_4, tail_5, tail_6, tail_7):
                    piece(t)
                tail_8(t, True)
                tables()

            def tables():
                dve.wait_ge(slots_ready, NT)
                dve.wait_ge(count_mm, 1)
                cnt, nblk, cum = M, ez, sg
                step(nc.vector.tensor_copy(cnt[:], pB[:, RNK:RNK + N_EXP]))
                step(nc.vector.tensor_scalar(nblk[:], cnt[:], 0.0, 1.0, ALU.mult, ALU.add))
                for j in range(1, T // P):
                    step(nc.vector.scalar_tensor_tensor(nblk[:], cnt[:], float(j * P), nblk[:], ALU.is_gt, ALU.add))
                step(nc.vector.tensor_scalar(rk[:], nblk[:], 0.0, 1.0, ALU.mult, ALU.add))
                step(nc.vector.tensor_tensor_scan(cum[:], rk[:], nblk[:], 0.0, ALU.mult, ALU.add))
                step(nc.vector.tensor_copy(cumi[:, RING + 1:RING + 1 + N_EXP], cum[:]))
                step(nc.vector.tensor_scalar(cumi[:, RING + 1 + N_EXP:], cumi[:, RING + N_EXP:RING + 1 + N_EXP], float(T // P), None, ALU.add))
                for c in range(2):
                    step(nc.vector.tensor_scalar(sm[:, 2 + c:3 + c], tok0[:], float(c * P), None, ALU.add))
                    step(nc.vector.tensor_scalar(rk[:], cum[:], sm[:, 2 + c:3 + c], None, ALU.is_le))
                    step(nc.vector.tensor_reduce(wk[:, c:c + 1], rk[:], AX.X, ALU.add))
                    step(nc.vector.tensor_tensor(rk[:], rk[:], nblk[:], ALU.mult))
                    step(nc.vector.tensor_reduce(wk[:, 2 + c:3 + c], rk[:], AX.X, ALU.add))
                    step(nc.vector.tensor_tensor(wk[:, 4 + c:5 + c], sm[:, 2 + c:3 + c], wk[:, 2 + c:3 + c], ALU.subtract))
                    step(nc.vector.scalar_tensor_tensor(wk[:, 4 + c:5 + c], wk[:, c:c + 1], float(NT), wk[:, 4 + c:5 + c], ALU.mult, ALU.add))
                    step(nc.vector.tensor_scalar(wk[:, 4 + c:5 + c], wk[:, 4 + c:5 + c], float((N_EXP + 1) * NT - 1), None, ALU.min))
                    nc.vector.tensor_copy(blk[:, c:c + 1], wk[:, 4 + c:5 + c]).then_inc(tables_ready, 1)
                    nc.vector.tensor_copy(blk[:, 2 + c:3 + c], wk[:, c:c + 1]).then_inc(tables_ready, 1)

            ext.update(trip=0, per=0, base=0, n=0)
            maxs(0, 0)
            scale_p(0, 0)
            trips(dve, trip, tail)

        @block.tensor
        def _(pe):
            pe.wait_ge(const_in, 16 * 7)
            ident, tri, ones = cst[:, 0, :], cst[:, 1, :], cst[:, 2, :]

            def scores(t, n, prev):
                if n != 1 and (n or prev):
                    pe.wait_ge(exp_ready, t * NHD + (n - 1))
                elif prev:
                    pe.wait_ge(f_ready, 2 * t)
                for h in range(2):
                    m = nc.tensor.matmul(pS[:, n % 2, h * 512:(h + 1) * 512], qs[:, n % GQ, :],
                                         kTp[:, n // GQ, bass.ds((t // KT) * SEQ + h * 512, 512)], start=True, stop=True)
                m.then_inc(s_mm, 1)

            def transposes(t, n, prev):
                pe.wait_ge(p_ready, t * NHD + (n + 1))
                for h, (done, copied) in enumerate(((t0_mm, t0_copied), (t1_mm, t1_copied))):
                    if prev or n:
                        pe.wait_ge(copied, t * NHD + n)
                    if prev and n == 5:
                        pe.wait_ge(ut_copied, 2 * t)
                    for k in range(4):
                        m = nc.tensor.transpose(pX[:, h, k * P:(k + 1) * P], pr[:, n % 2, (4 * h + k) * P:(4 * h + k + 1) * P], ident)
                    m.then_inc(done, 1)

            def values(t, g, prev):
                pe.wait_ge(t0_copied, t * NHD + GQ * (g + 1))
                pe.wait_ge(v_ready, t + 1)
                pe.wait_ge(t1_copied, t * NHD + GQ * (g + 1))
                if prev and g == 0:
                    pe.wait_ge(att_scaled, t)
                    pe.wait_ge(asq_ready, t)
                for k in range(KT):
                    m = nc.tensor.matmul(pO[g * HD:(g + 1) * HD, :, :], vs[:, k, g * HD:(g + 1) * HD], pT[:, k, :, :], start=(k == 0), stop=(k == KT - 1))
                m.then_inc(pv_mm, 1)

            def squares(col, src, done):
                for i in range(GQ):
                    m = nc.tensor.matmul(pB[:, col:col + 1], src[:, i, :], ones[:, 0:1], start=(i == 0), stop=(i == GQ - 1))
                m.then_inc(done, 1)

            def to_rows(col, which, done):
                nc.tensor.matmul(pB[:, col:col + P], ones, diag[:, which, :], start=True, stop=True).then_inc(done, 1)

            def project(which, h, src):
                for i in range(GQ):
                    m = nc.tensor.matmul(pS[:, 1, h * 512:(h + 1) * 512], src[:, i, :], wo[:, which, i, h * 512:(h + 1) * 512],
                                         start=(which == 1 and i == 0), stop=(which == 0 and i == GQ - 1))
                return m

            def tail_u(t, heads):
                pe.wait_ge(u2_ready, t)
                pe.wait_ge(t0_copied, heads)
                pe.wait_ge(t1_copied, heads)
                for k in range(KD):
                    m = nc.tensor.transpose(pX[:, k // 4, (k % 4) * P:(k % 4 + 1) * P], f[:, k * P:(k + 1) * P], ident)
                m.then_inc(ut_mm, 1)

            def tail_l(t):
                pe.wait_ge(ut_copied, 2 * t)
                for k in range(KD):
                    m = nc.tensor.matmul(pB[:, LOG:LOG + N_EXP], uT[:, k, :], wr[:, k, :], start=(k == 0), stop=(k == KD - 1))
                m.then_inc(log_mm, 1)

            def tail_r(t):
                pe.wait_ge(m_ready, t)
                nc.tensor.matmul(pB[:, RNK:RNK + N_EXP], tri, M[:], start=True, stop=False)
                nc.tensor.matmul(pB[:, RNK:RNK + N_EXP], ones, Msum[:], start=False, stop=True).then_inc(rank_mm, 1)

            def trip(t, prev, nxt):
                scores(t, 1, prev)
                for n in range(NHD):
                    transposes(t, n, prev)
                    if n == 1:
                        pe.wait_ge(lsq_ready, t + 1)
                        if prev:
                            pe.wait_ge(att_scaled, t)
                            pe.wait_ge(rank_read, t)
                        squares(SSL, lsq, ssl_mm)
                    if n == 3:
                        pe.wait_ge(diag_ready, 2 * t + 1)
                        to_rows(BCL, 1, rows_mm)
                        scores(t, 5, prev)
                        values(t, 0, prev)
                    elif n + 2 < NHD:
                        scores(t, n + 2, prev)
                    elif nxt and n == 6:
                        pe.wait_ge(q_ready, t + 2)
                        scores(t + 1, 0, 1)
                    if prev and n == 4:
                        tail_u(t, t * NHD + 5)
                    if prev and n == 5:
                        pe.wait_ge(bcl_read, t + 1)
                        tail_l(t)
                values(t, 1, prev)
                pe.wait_ge(asq_ready, t + 1)
                pe.wait_ge(bcl_read, t + 1)
                if prev:
                    pe.wait_ge(ez_ready, t)
                squares(SSA, asq, ssa_mm)
                pe.wait_ge(l_ready, t + 1)
                pe.wait_ge(exp_ready, (t + 1) * NHD)
                if not prev:
                    pe.wait_ge(wo_in, 16)
                project(1, 0, ls)
                pe.wait_ge(diag_ready, 2 * t + 2)
                to_rows(BCA, 0, rows_mm)
                project(1, 1, ls).then_inc(p2_mm, 1)
                pe.wait_ge(att_scaled, t + 1)
                project(0, 0, aT)
                project(0, 1, aT).then_inc(p1_mm, 1)
                if prev:
                    tail_r(t)

            def tail(t):
                tail_u(t, t * NHD)
                pe.wait_ge(ssa_read, t)
                pe.wait_ge(rank_read, t)
                tail_l(t)
                pe.wait_ge(ez_ready, t)
                tail_r(t)
                pe.wait_ge(slots_ready, NT)
                nc.tensor.matmul(pB[:, RNK:RNK + N_EXP], ones, Msum[:], start=True, stop=True).then_inc(count_mm, 1)

            pe.wait_ge(q_ready, 1)
            scores(0, 0, 0)
            trips(pe, trip, tail)


def experts(nc, u2_d, list_d, acc_d, count_d, block_d, w_exp_in, w_exp_out, w_sh_in, w_sh_out, ident_d, apart):
    FH = 2 * D_E
    FC = D_E // P
    NS = T // P
    with ExitStack() as ctx:
        sb = lambda n, s, d=F32: ctx.enter_context(nc.sbuf_tensor(n, s, d))
        ps = lambda n, s: ctx.enter_context(nc.psum_tensor(n, s, F32))
        sem = lambda n: ctx.enter_context(nc.semaphore("ex_" + n))
        wi = sb("ex_wi", [P, RING, KD, FH])
        wo = sb("ex_wo", [P, RING, FC, D])
        ident = sb("ex_ident", [P, P])
        brow = sb("ex_brow", [P, 2], I32)
        raw = sb("ex_raw", [P, 2, P, 2], I32)
        tokf = sb("ex_tokf", [P, 2, P])
        tok = sb("ex_tok", [P, 2 * P], I32)
        wgt = sb("ex_wgt", [P, 2 * P])
        gidx = sb("ex_gidx", [P, 1], I32)
        sidx = sb("ex_sidx", [P, 1], I32)
        xg = sb("ex_xg", [P, D])
        xT = sb("ex_xT", [P, KD, P])
        sl = sb("ex_silu", [P, D_E])
        hg = sb("ex_h", [P, D_E])
        hT = sb("ex_hT", [P, FC, P])
        y = sb("ex_y", [P, D])
        pX = ps("ex_pX", [P, 2, 512])
        pH = ps("ex_pH", [P, 512])
        pG = ps("ex_pG", [P, 512])
        pY = ps("ex_pY", [P, 2, 512])

        const_in, raw_in, tokf_ready, entries_mm, entries_ready = (sem("const_in"), sem("raw_in"), sem("tokf_ready"),
                                                                           sem("entries_mm"), sem("entries_ready"))
        gidx_ready, gathered, sidx_ready, scattered, y_free = sem("gidx_ready"), sem("gathered"), sem("sidx_ready"), sem("scattered"), sem("y_free")
        w_in, w_ready = [sem(f"w_in{r}") for r in range(RING)], sem("w_ready")
        x_mm, x0_copied, x1_copied, h_mm, silu_ready, h_ready, g_mm, g_copied, y_mm, y0_ready, y1_ready = (
            sem("x_mm"), sem("x0_copied"), sem("x1_copied"), sem("h_mm"), sem("silu_ready"), sem("h_ready"), sem("g_mm"), sem("g_copied"),
            sem("y_mm"), sem("y0_ready"), sem("y1_ready"))
        block = ctx.enter_context(nc.Block())
        MAXB = N_EXP + T * TOP_K // P

        def total(eng):
            return eng.value_load(count_d[:, RING + N_EXP + 1:RING + N_EXP + 2], min_val=N_EXP + NS, max_val=MAXB + NS)

        @block.sync
        def _(sp):
            sp.sem_inc(w_in[RING - 1], 32)
            sp.dma_start(brow[:], block_d[:, 0:2 * P].rearrange("a (c p) -> p (a c)", p=P), allow_slow_non_contiguous=True).then_inc(const_in, 16)
            sp.dma_start(ident[:], ident_d).then_inc(const_in, 16)

            def load(r, src_in, src_out):
                sp.dma_start(wi[:, r, :, :], src_in).then_inc(w_in[r], 16)
                sp.dma_start(wo[:, r, :, :], src_out).then_inc(w_in[r], 16)

            with sp.Fori(0, N_EXP // RING) as q:
                for r in range(RING):
                    done = sp.value_load(count_d[:, bass.ds(q * RING + (r + 1), 1)], min_val=0, max_val=MAXB)
                    sp.wait_ge(y_mm, done + 1)
                    load(r, w_exp_in[bass.ds(q * RING + r, 1)].rearrange("a (k p) f -> p (a k) f", p=P),
                         w_exp_out[bass.ds(q * RING + r, 1)].rearrange("a (c p) d -> p (a c) d", p=P))
                    sp.wait_ge(w_in[(r - 1) % RING], q * 32 + 32)
                    sp.sem_inc(w_ready, 1)
            done = sp.value_load(count_d[:, N_EXP + 1:N_EXP + 2], min_val=0, max_val=MAXB)
            sp.wait_ge(y_mm, done + 1)
            load(0, w_sh_in.rearrange("(k p) f -> p k f", p=P), w_sh_out.rearrange("(c p) d -> p c d", p=P))
            sp.wait_ge(w_in[RING - 1], (N_EXP // RING + 1) * 32)
            sp.sem_inc(w_ready, 1)
            sp.wait_ge(w_in[0], (N_EXP // RING + 1) * 32)
            sp.sem_inc(w_ready, 1)

        @block.gpsimd
        def _(pool):
            n = total(pool)

            pool.wait_ge(const_in, 32)
            for c in range(2):
                nc.gpsimd.indirect_dma_start(raw[:, c, :, :].rearrange("p t c -> p (t c)"), None, list_d.rearrange("(b t) c -> b (t c)", t=P),
                                             bass.IndirectOffsetOnAxis(ap=brow[:, c:c + 1].bitcast(U32), axis=0)).then_inc(raw_in, 16)
            pool.wait_ge(entries_ready, 2)

            def gather(b, first=False):
                pool.wait_ge(x_mm, b + 1)
                if not first:
                    pool.wait_ge(gathered, b * 16)
                passed(pool, apart)
                nc.gpsimd.tensor_copy(gidx[:], tok[:, bass.ds(b, 1)]).then_inc(gidx_ready, 1)
                pool.wait_ge(gidx_ready, b + 1)
                passed(pool, apart)
                nc.gpsimd.indirect_dma_start(xg[:], None, u2_d, bass.IndirectOffsetOnAxis(ap=gidx[:].bitcast(U32), axis=0)).then_inc(gathered, 16)

            for b in range(4):
                gather(b, b == 0)
            with pool.Fori(0, n) as b:
                nc.gpsimd.tensor_copy(sidx[:], tok[:, bass.ds(b, 1)]).then_inc(sidx_ready, 1)
                pool.wait_ge(sidx_ready, b + 1)
                pool.wait_ge(y0_ready, b + 2)
                pool.wait_ge(y1_ready, b + 2)
                passed(pool, apart)
                nc.gpsimd.indirect_dma_start(acc_d, bass.IndirectOffsetOnAxis(ap=sidx[:].bitcast(U32), axis=0), y[:], None,
                                             compute_op=ALU.add).then_inc(scattered, 16)
                gather(b + 4)
                pool.wait_ge(scattered, b * 16 + 16)
                pool.sem_inc(y_free, 1)
            pool.wait_ge(gathered, n * 16 + 64)
            passed(pool, apart)
            pool.wait_ge(scattered, n * 16)

        @block.scalar
        def _(act):
            n = total(act)

            def copy_x(b):
                act.wait_ge(x_mm, b + 2)
                act.wait_ge(h_mm, b + 1)
                nc.scalar.activation(xT[:, 0:4, :], pX[:, 0, :].rearrange("p (k t) -> p k t", t=P), ACT.Copy).then_inc(x0_copied, 1)

            def silu(b):
                act.wait_ge(h_mm, b + 2)
                nc.scalar.activation(sl[:], pH[:, 0:D_E], ACT.Silu).then_inc(silu_ready, 1)

            act.wait_ge(entries_mm, 2)
            nc.scalar.activation(wgt[:], pX[:, 1, 0:2 * P], ACT.Copy).then_inc(entries_ready, 1)
            copy_x(0)
            silu(0)
            copy_x(1)
            with act.Fori(0, n) as b:
                act.wait_ge(h_ready, b + 1)
                silu(b + 1)
                act.wait_ge(g_mm, b + 1)
                nc.scalar.activation(hT[:], pG[:, 0:FC * P].rearrange("p (c t) -> p c t", t=P), ACT.Copy).then_inc(g_copied, 1)
                copy_x(b + 2)
                act.wait_ge(y_mm, b + 2)
                act.wait_ge(y_free, b + 1)
                nc.scalar.activation(y[:, 0:512], pY[:, 0, :], ACT.Copy, scale=wgt[:, bass.ds(b, 1)]).then_inc(y0_ready, 1)

        @block.vector
        def _(dve):
            n = total(dve)

            def copy_x(b):
                dve.wait_ge(x_mm, b + 2)
                dve.wait_ge(h_mm, b + 1)
                nc.vector.tensor_copy(xT[:, 4:8, :], pX[:, 1, :].rearrange("p (k t) -> p k t", t=P)).then_inc(x1_copied, 1)

            def gate(b):
                dve.wait_ge(silu_ready, b + 1)
                nc.vector.tensor_tensor(hg[:], sl[:], pH[:, D_E:FH], ALU.mult).then_inc(h_ready, 1)

            dve.wait_ge(raw_in, 32)
            nc.vector.tensor_copy(tokf[:], raw[:, :, :, 0]).then_inc(tokf_ready, 1)
            dve.wait_ge(entries_mm, 2)
            nc.vector.tensor_copy(tok[:], pX[:, 0, 0:2 * P]).then_inc(entries_ready, 1)
            copy_x(0)
            gate(0)
            copy_x(1)
            with dve.Fori(0, n) as b:
                dve.wait_ge(g_mm, b + 1)
                gate(b + 1)
                copy_x(b + 2)
                dve.wait_ge(y_mm, b + 2)
                dve.wait_ge(y_free, b + 1)
                nc.vector.tensor_scalar(y[:, 512:], pY[:, 1, :], wgt[:, bass.ds(b, 1)], None, ALU.mult).then_inc(y1_ready, 1)

        @block.tensor
        def _(pe):
            pe.sem_inc(x_mm, 1)
            pe.sem_inc(h_mm, 1)
            pe.sem_inc(y_mm, 1)
            pe.sem_inc(y_free, 1)
            pe.sem_inc(y0_ready, 1)
            pe.sem_inc(y1_ready, 1)
            pe.wait_ge(const_in, 32)
            pe.wait_ge(raw_in, 32)
            for c in range(2):
                m = nc.tensor.transpose(pX[:, 1, c * P:(c + 1) * P], raw[:, c, :, 1].bitcast(F32), ident[:])
            m.then_inc(entries_mm, 1)
            pe.wait_ge(tokf_ready, 1)
            for c in range(2):
                m = nc.tensor.transpose(pX[:, 0, c * P:(c + 1) * P], tokf[:, c, :], ident[:])
            m.then_inc(entries_mm, 1)
            pe.wait_ge(entries_ready, 2)

            def expert_of(b):
                return pe.value_load(block_d[:, bass.ds(b + 2 * P, 1)], min_val=0, max_val=N_EXP)

            def transpose_x(b):
                pe.wait_ge(gathered, b * 16 + 16)
                if not isinstance(b, int) or b > 0:
                    pe.wait_ge(x0_copied, b)
                    pe.wait_ge(x1_copied, b)
                for k in range(KD):
                    m = nc.tensor.transpose(pX[:, k // 4, (k % 4) * P:(k % 4 + 1) * P], xg[:, k * P:(k + 1) * P], ident[:])
                m.then_inc(x_mm, 1)

            def first(b, e):
                pe.wait_ge(w_ready, e + 2)
                pe.wait_ge(x0_copied, b + 1)
                pe.wait_ge(x1_copied, b + 1)
                slot = e % RING
                for k in range(KD):
                    m = nc.tensor.matmul(pH[:], xT[:, k, :], wi[:, bass.ds(slot, 1), k, :].rearrange("p a f -> p (a f)"),
                                         start=(k == 0), stop=(k == KD - 1))
                m.then_inc(h_mm, 1)

            transpose_x(0)
            first(0, expert_of(0))
            transpose_x(1)
            n = total(pe)
            with pe.Fori(0, n) as b:
                ahead = expert_of(b + 1)
                pe.wait_ge(h_ready, b + 1)
                first(b + 1, ahead)
                for c in range(FC):
                    m = nc.tensor.transpose(pG[:, c * P:(c + 1) * P], hg[:, c * P:(c + 1) * P], ident[:])
                m.then_inc(g_mm, 1)
                transpose_x(b + 2)
                now = expert_of(b)
                pe.wait_ge(g_copied, b + 1)
                pe.wait_ge(y0_ready, b + 1)
                pe.wait_ge(y1_ready, b + 1)
                slot = now % RING
                for h in range(2):
                    for c in range(FC):
                        m = nc.tensor.matmul(pY[:, h, :], hT[:, c, :], wo[:, bass.ds(slot, 1), c, h * 512:(h + 1) * 512].rearrange("p a d -> p (a d)"),
                                             start=(c == 0), stop=(c == FC - 1))
                m.then_inc(y_mm, 1)
            pe.wait_ge(gathered, n * 16 + 48)
            pe.sem_inc(x_mm, 1)


def output(nc, x1_d, acc_d, mod_d, ln2_rows, y_d, apart):
    with ExitStack() as ctx:
        sb = lambda n, s, d=F32: ctx.enter_context(nc.sbuf_tensor(n, s, d))
        sem = lambda n: ctx.enter_context(nc.semaphore("out_" + n))
        NBUF = 8
        ln = sb("out_ln", [P, 2, D])
        gate = sb("out_gate", [P, NB, D])
        half = sb("out_half", [P, 1])
        x1 = sb("out_x1", [P, NBUF, D])
        ac = sb("out_acc", [P, NBUF, D])
        st = sb("out_st", [P, NBUF, 2, 6])
        mv = sb("out_mv", [P, NBUF, 2])
        ve = sb("out_ve", [P, NBUF])
        rstd = sb("out_rstd", [P, NBUF])
        nmr = sb("out_nmr", [P, NBUF])
        const_in, once, gated, var_ready, rstd_ready, nmr_ready, normed, scaled, done, steps = (
            sem("const_in"), sem("once"), sem("gated"), sem("var_ready"), sem("rstd_ready"), sem("nmr_ready"), sem("normed"), sem("scaled"), sem("done"),
            sem("steps"))
        loaded, stored = [sem(f"loaded{i}") for i in range(NBUF)], [sem(f"stored{i}") for i in range(NBUF)]
        block = ctx.enter_context(nc.Block())
        GB = NT // NB // NBUF

        @block.sync
        def _(sp):
            sp.dma_start(ln[:], ln2_rows.partition_broadcast(P)).then_inc(const_in, 16)
            sp.dma_start(gate[:], mod_d[:, (N_MOD - 1) * D:].partition_broadcast(P)).then_inc(const_in, 16)
            for i in range(NBUF):
                sp.sem_inc(stored[i], 16)
            with sp.Fori(0, NT // NBUF) as g:
                for i in range(NBUF):
                    sp.wait_ge(stored[i], g * 16 + 16)
                    tok = bass.ds(g * NBUF * P + i * P, P)
                    sp.dma_start(ac[:, i, :], acc_d[tok, :]).then_inc(loaded[i], 16)
                    sp.dma_start(x1[:, i, :], x1_d[tok, :]).then_inc(loaded[i], 16)

        @block.gpsimd
        def _(pool):
            nc.gpsimd.memset(half[:], -0.5).then_inc(once, 1)
            pool.wait_ge(once, 1)
            pool.wait_ge(const_in, 32)
            with pool.Fori(0, NT // NBUF) as g:
                for i in range(NBUF + 1):
                    if i < NBUF:
                        pool.wait_ge(loaded[i], g * 32 + 32)
                        passed(pool, apart)
                        nc.gpsimd.tensor_tensor(ac[:, i, :], ac[:, i, :], gate[:, bass.ds(g // GB, 1), :].rearrange("p a d -> p (a d)"), ALU.mult).then_inc(gated, 1)
                    if i:
                        pool.wait_ge(var_ready, g * NBUF + i)
                        nc.gpsimd.tensor_tensor(rstd[:, i - 1:i], ve[:, i - 1:i], half[:], ALU.pow).then_inc(rstd_ready, 1)

        @block.vector
        def _(dve):
            dve.wait_ge(const_in, 32)
            with dve.Fori(0, NT // NBUF) as g:
                step = Chain(dve, steps, g, NBUF * 3)
                for i in range(NBUF + 1):
                    if i < NBUF:
                        n = g * NBUF + (i + 1)
                        dve.wait_ge(loaded[i], g * 32 + 32)
                        dve.wait_ge(gated, n)
                        step(nc.vector.scalar_tensor_tensor(x1[:, i, :], x1[:, i, :], ALPHA, ac[:, i, :], ALU.mult, ALU.add))
                        for c in range(2):
                            s = nc.vector.bn_stats(st[:, i, c, :], x1[:, i, c * 512:(c + 1) * 512])
                        step(s)
                        passed(dve, apart)
                        step(nc.vector.bn_aggr(mv[:, i, :], st[:, i, :, :].rearrange("p a s -> p (a s)")))
                        nc.vector.tensor_scalar(ve[:, i:i + 1], mv[:, i, 1:2], EPS, None, ALU.add).then_inc(var_ready, 1)
                    if i:
                        dve.wait_ge(normed, n - 1 if i < NBUF else n)
                        nc.vector.tensor_tensor(x1[:, i - 1, :], x1[:, i - 1, :], ln[:, 0, :], ALU.mult).then_inc(scaled, 1)
                        dve.wait_ge(scaled, n - 1 if i < NBUF else n)
                        nc.vector.tensor_tensor(x1[:, i - 1, :], x1[:, i - 1, :], ln[:, 1, :], ALU.add).then_inc(done, 1)
                    if i < NBUF:
                        dve.wait_ge(rstd_ready, n)
                        nc.vector.scalar_tensor_tensor(nmr[:, i:i + 1], mv[:, i, 0:1], -1.0, rstd[:, i:i + 1], ALU.mult, ALU.mult).then_inc(nmr_ready, 1)
                step.closed()

        @block.scalar
        def _(act):
            with act.Fori(0, NT // NBUF) as g:
                for i in range(NBUF + 1):
                    n = g * NBUF + (i + 1)
                    if i < NBUF:
                        act.wait_ge(nmr_ready, n)
                        nc.scalar.activation(x1[:, i, :], x1[:, i, :], ACT.Identity, bias=nmr[:, i:i + 1], scale=rstd[:, i:i + 1]).then_inc(normed, 1)
                    if i:
                        act.wait_ge(done, n - 1)
                        act.dma_start(y_d[bass.ds(g * NBUF * P + (i - 1) * P, P), :], x1[:, i - 1, :]).then_inc(stored[i - 1], 16)
            for i in range(NBUF):
                act.wait_ge(stored[i], 16 * (NT // NBUF + 1))


def program(nc, a, scratch, y_d):
    mod_d = scratch("s_mod", (NB, N_MOD * D), F32)
    xl_d, gl_d = scratch("s_xl", (D_LRU, T), F32), scratch("s_gl", (D_LRU, T), F32)
    x1_d, u2_d, acc_d = scratch("s_x1", (T, D), F32), scratch("s_u2", (T + P, D), F32), scratch("s_acc", (T + P, D), F32)
    list_d = scratch("s_list", ((N_EXP + 1) * T, 2), I32)
    count_d, block_d = scratch("s_count", (1, CUMS), I32), scratch("s_block", (1, 4 * P), I32)
    conditioning(nc, a["w_ada"], a["b_ada"], a["cT"], mod_d, list_d, acc_d, u2_d)
    shared = ExitStack()
    apart = shared.enter_context(nc.semaphore("apart"))
    with ExitStack() as ctx:
        sb = lambda n, s, d=F32: ctx.enter_context(nc.sbuf_tensor(n, s, d))
        keep = (sb("qT", [P, NQ // NKV, T]), sb("kTp", [P, NKV, T]), sb("v", [P, NT, NKV * HD]))
        mod_cols = mod_d.rearrange("b (m k p) -> b p m k", k=KD, p=P)[:, :, 0:2, :]
        input_projection(nc, a["x"], a["w_in"], mod_cols, a["rope"], a["qk_gain"], a["consts"][:, 0, :], xl_d, gl_d, keep, apart)
        lruT = sb("lruT", [P, KL, T])
        rg_lru(nc, xl_d, gl_d, a["gate_w"], a["chan"], lruT, apart)
        attention_tiles(nc, a["x"], mod_d, a["ln1"], a["w_out"], a["w_router"], a["router_bias"], a["chan_gain"],
                        (a["consts"], a["iota"], a["token"]), x1_d, u2_d, keep, lruT, (list_d, acc_d, count_d, block_d), apart)
    experts(nc, u2_d, list_d, acc_d, count_d, block_d, a["w_exp_in"], a["w_exp_out"], a["w_sh_in"], a["w_sh_out"], a["consts"][:, 0, :], apart)
    output(nc, x1_d, acc_d, mod_d, a["ln2"], y_d, apart)
    shared.close()


def rope_tables():
    t = np.arange(SEQ)
    inv = np.float32(10000.0) ** (-np.arange(ROPE_FREQS, dtype=np.float32) / ROPE_FREQS)
    ang = np.stack([(t // GRID_W)[:, None] * inv, (t % GRID_W)[:, None] * inv], axis=1).astype(np.float32)
    cos = np.repeat(np.cos(ang)[:, :, None], 2, axis=2).reshape(SEQ, HD)
    sin = np.stack([-np.sin(ang), np.sin(ang)], axis=2).reshape(SEQ, HD)
    return np.ascontiguousarray(np.stack([cos, sin], 1).reshape(SEQ // P, P, 2, HD).transpose(1, 0, 2, 3).astype(np.float32))


def layout(i):
    w = {k: np.asarray(v)[0] for k, v in i.items() if not k.startswith(("x_", "c_"))}
    G = NQ // NKV
    gate_w = np.zeros((KL, P, 4, P), np.float32)
    for c in range(KL):
        for d in range(2):
            for g, name in enumerate(("lru_wa", "lru_wx")):
                for s in range(2):
                    gate_w[c, 64 * s:64 * s + 64, 2 * d + g, 64 * s:64 * s + 64] = w[name][d, 2 * c + s]
    per_chan = lambda a: a.reshape(-1, KL, P).transpose(1, 2, 0)
    out = {
        "x": np.concatenate([np.asarray(i["x_prompt"]), np.asarray(i["x_sample"])], 0).reshape(T, D),
        "cT": np.concatenate([np.asarray(i["c_prompt"]), np.asarray(i["c_sample"])], 0).reshape(NB, KD, P).transpose(2, 1, 0),
        "w_ada": w["w_ada"], "b_ada": w["b_ada"].reshape(1, -1), "w_in": w["w_in"],
        "qk_gain": np.concatenate([np.tile(w["q_norm_g"], NQ), np.tile(w["k_norm_g"], NKV)]),
        "gate_w": gate_w,
        "chan": np.concatenate([per_chan(w["conv_w"]), per_chan(w["conv_b"][None]), per_chan(w["lru_ba"]), per_chan(w["lru_bx"]),
                                per_chan(w["lru_lambda"])], 2),
        "chan_gain": np.stack([w["attn_out_g"].reshape(NKV, G, HD).transpose(0, 2, 1).reshape(P, G), w["lru_out_g"].reshape(KL, P).T], 1),
        "w_out": np.stack([w["w_out"][:D_ATT].reshape(NKV, G, HD, D).transpose(0, 2, 1, 3).reshape(P, G, D),
                           w["w_out"][D_ATT:].reshape(KL, P, D).transpose(1, 0, 2)], 1),
        "w_router": w["w_router"].reshape(KD, P, N_EXP).transpose(1, 0, 2), "router_bias": w["router_bias"],
        "ln1": np.stack([w["ln1_g"], w["ln1_b"]]), "ln2": np.stack([w["ln2_g"], w["ln2_b"]]),
        "w_exp_in": w["w_exp_in"], "w_exp_out": w["w_exp_out"], "w_sh_in": w["w_sh_in"], "w_sh_out": w["w_sh_out"],
        "rope": rope_tables(),
        "consts": np.stack([np.eye(P), np.triu(np.ones((P, P)), 1), np.ones((P, P))], 1).astype(np.float32),
        "iota": np.arange(N_EXP, dtype=np.float32), "token": np.arange(P, dtype=np.float32).reshape(P, 1),
    }
    return {k: np.ascontiguousarray(v) for k, v in out.items()}


def kernel(**inputs):
    import concourse.bacc as bacc
    from concourse.bass_utils import run_bass_kernel_spmd

    nc = bacc.Bacc("TRN2", target_bir_lowering=False, num_devices=1)
    arrays = {"in_" + k: v for k, v in layout(inputs).items()}
    args = {k[3:]: nc.dram_tensor(k, v.shape, mybir.dt.from_np(v.dtype), kind="ExternalInput").ap() for k, v in arrays.items()}
    y = nc.dram_tensor("y", (T, D), F32, kind="ExternalOutput").ap()
    program(nc, args, lambda n, s, d: nc.dram_tensor(n, s, d, kind="Internal").ap(), y)
    got = run_bass_kernel_spmd(nc, [arrays], core_ids=[0]).results[0]["y"]
    return got[:SEQ].reshape(1, SEQ, D), got[SEQ:].reshape(1, SEQ, D)
```
